# Optimizing a Trainium2 kernel written in Bass

```python
import math
import jax, jax.numpy as jnp
from jax import lax
import numpy as np

D_MODEL = 1024
BATCH = 1
SEQ = 1024
DEPTH = 1

HG_HEADS = 4
HG_DK = 128
HG_DV = 128
HG_W = HG_HEADS * HG_DK
HG_VW = HG_HEADS * HG_DV
HG_CHUNK = 64
SB_HEADS = 8
SB_DH = 64
SB_W = SB_HEADS * SB_DH
DA_HEADS = 4
DA_DH = 64
DA_DV = 2 * DA_DH
DA_QK = DA_HEADS * 2 * DA_DH
DA_W = DA_HEADS * DA_DV
REL_BUCKETS = 32
REL_MAX_DIST = 128
D_FF = 2816
CONV_W = 3
Q_BLOCK = 128
N_BRANCH = 3
RMS_EPS = 1e-6

IN_SPLITS = (HG_W, HG_W, HG_VW, HG_VW,
             SB_W, SB_W, SB_W,
             DA_QK, DA_QK, DA_W,
             N_BRANCH * D_MODEL)
IN_WIDTH = sum(IN_SPLITS)

kernel_name = 'hybrid_hgrn2_stickbreak_diffattn_block'

def _rmsnorm(x, w):
    xf = x.astype(jnp.float32)
    y = xf * lax.rsqrt(jnp.mean(xf * xf, axis=-1, keepdims=True) + RMS_EPS)
    return (y * w.astype(jnp.float32)).astype(x.dtype)

def _split_cols(z):
    idx = np.cumsum(IN_SPLITS)[:-1].tolist()
    return jnp.split(z, idx, axis=-1)

def _to_heads(a, n_heads):
    b, s, w = a.shape
    return a.reshape(b, s, n_heads, w // n_heads).transpose(0, 2, 1, 3)

def _from_heads(a):
    b, h, s, d = a.shape
    return a.transpose(0, 2, 1, 3).reshape(b, s, h * d)

def _blocks_first(a, axis):
    s = a.shape[axis]
    a = a.reshape(a.shape[:axis] + (s // Q_BLOCK, Q_BLOCK) + a.shape[axis + 1:])
    return jnp.moveaxis(a, axis, 0)

def _blocks_merge(o):
    nb, b, h, qb, d = o.shape
    return jnp.moveaxis(o, 0, 2).reshape(b, h, nb * qb, d)

def _t5_bucket(dist):
    n = jnp.maximum(dist, 0)
    max_exact = REL_BUCKETS // 2
    scaled = jnp.log(jnp.maximum(n, 1).astype(jnp.float32) / max_exact) / math.log(REL_MAX_DIST / max_exact)
    large = jnp.minimum(max_exact + (scaled * (REL_BUCKETS - max_exact)).astype(jnp.int32), REL_BUCKETS - 1)
    return jnp.where(n < max_exact, n, large)

def _lambda_init(layer_idx):
    return 0.8 - 0.6 * math.exp(-0.3 * layer_idx)

def hgrn2_mixer(q, f_logit, i, g, lb, onorm_w):
    b, s, _ = q.shape
    lbf = lb.astype(jnp.float32)
    zf = f_logit.astype(jnp.float32)
    log_f = jnp.logaddexp(jnp.log(lbf), jnp.log1p(-lbf) + jax.nn.log_sigmoid(zf))
    key = (1.0 - lbf) * jax.nn.sigmoid(-zf)
    qh = _to_heads(q.astype(jnp.float32) * HG_DK ** -0.5, HG_HEADS)
    kh = _to_heads(key, HG_HEADS)
    gh = _to_heads(log_f, HG_HEADS)
    vh = _to_heads(i.astype(jnp.float32), HG_HEADS)
    n = s // HG_CHUNK

    def chunks(a):
        return jnp.moveaxis(a.reshape(b, HG_HEADS, n, HG_CHUNK, a.shape[-1]), 2, 0)

    causal = jnp.tril(jnp.ones((HG_CHUNK, HG_CHUNK), dtype=bool))[:, :, None]

    def step(state, inp):
        qc, kc, vc, gc = inp
        cum = jnp.cumsum(gc, axis=2)
        o_inter = jnp.einsum('bhtk,bhkv->bhtv', qc * jnp.exp(cum), state)
        rel = jnp.where(causal, cum[:, :, :, None, :] - cum[:, :, None, :, :], -jnp.inf)
        scores = jnp.einsum('bhtk,bhtsk,bhsk->bhts', qc, jnp.exp(rel), kc)
        o = o_inter + jnp.einsum('bhts,bhsv->bhtv', scores, vc)
        last = cum[:, :, -1:, :]
        state = (jnp.exp(last[:, :, 0, :, None]) * state
                 + jnp.einsum('bhsk,bhsv->bhkv', kc * jnp.exp(last - cum), vc))
        return state, o

    state0 = jnp.zeros((b, HG_HEADS, HG_DK, HG_DV), jnp.float32)
    _, o = lax.scan(step, state0, (chunks(qh), chunks(kh), chunks(vh), chunks(gh)))
    o = jnp.moveaxis(o, 0, 2).reshape(b, HG_HEADS, s, HG_DV)
    o = _rmsnorm(o, onorm_w)
    return _from_heads(o) * jax.nn.silu(g.astype(jnp.float32))

def stick_breaking_mixer(q, k, v):
    s = q.shape[1]
    qh, kh, vh = _to_heads(q, SB_HEADS), _to_heads(k, SB_HEADS), _to_heads(v, SB_HEADS)
    pos = jnp.arange(s)

    def block(args):
        qb, t0 = args
        z = jnp.einsum('bhqd,bhkd->bhqk', qb, kh).astype(jnp.float32) * SB_DH ** -0.5
        t = t0 + jnp.arange(Q_BLOCK)
        mask = pos[None, :] < t[:, None]
        log_1mb = jnp.where(mask, jax.nn.log_sigmoid(-z), 0.0)
        later = lax.cumsum(log_1mb, axis=3, reverse=True) - log_1mb
        w = jnp.where(mask, jnp.exp(jax.nn.log_sigmoid(z) + later), 0.0)
        return jnp.einsum('bhqk,bhkd->bhqd', w.astype(vh.dtype), vh)

    starts = jnp.arange(s // Q_BLOCK, dtype=jnp.int32) * Q_BLOCK
    o = lax.map(block, (_blocks_first(qh, 2), starts))
    return _from_heads(_blocks_merge(o))

def diff_attention_mixer(q, k, v, lam, onorm_w, rel_bias, lam_init):
    b, s, _ = q.shape
    qh = q.reshape(b, s, DA_HEADS, 2, DA_DH).transpose(0, 2, 3, 1, 4)
    kh = k.reshape(b, s, DA_HEADS, 2, DA_DH).transpose(0, 2, 3, 1, 4)
    vh = _to_heads(v, DA_HEADS)
    lamf = lam.astype(jnp.float32)
    lam_full = jnp.exp(jnp.sum(lamf[0] * lamf[1])) - jnp.exp(jnp.sum(lamf[2] * lamf[3])) + lam_init
    table = rel_bias.astype(jnp.float32)
    pos = jnp.arange(s)

    def block(args):
        qb, t0 = args
        t = t0 + jnp.arange(Q_BLOCK)
        dist = t[:, None] - pos[None, :]
        bias = jnp.transpose(table[_t5_bucket(dist)], (2, 0, 1))[None, :, None]
        logits = jnp.einsum('bhmqd,bhmkd->bhmqk', qb, kh).astype(jnp.float32) * DA_DH ** -0.5 + bias
        logits = jnp.where(dist >= 0, logits, -jnp.inf)
        p = jax.nn.softmax(logits, axis=-1)
        w = p[:, :, 0] - lam_full * p[:, :, 1]
        return jnp.einsum('bhqk,bhkd->bhqd', w.astype(vh.dtype), vh)

    starts = jnp.arange(s // Q_BLOCK, dtype=jnp.int32) * Q_BLOCK
    o = _blocks_merge(lax.map(block, (_blocks_first(qh, 3), starts)))
    o = _rmsnorm(o, onorm_w) * (1.0 - lam_init)
    return _from_heads(o)

def conv_glu_ffn(h, w_up, conv_w, conv_b, w_down):
    u = h @ w_up
    s = u.shape[1]
    up = jnp.pad(u, ((0, 0), (CONV_W - 1, 0), (0, 0)))
    u = conv_b + sum(up[:, j:j + s] * conv_w[j] for j in range(CONV_W))
    gate, val = jnp.split(u, 2, axis=-1)
    return (jax.nn.silu(gate) * val) @ w_down

def setup_inputs(seed: int = 0) -> dict:
    key = jax.random.key(seed)
    ks = jax.random.split(key, 18)

    def nrm(k, shape, scale):
        return jax.random.normal(k, shape, jnp.float32) * scale

    ff2 = 2 * D_FF
    return {
        'x': nrm(ks[0], (BATCH, SEQ, D_MODEL), 1.0),
        'attn_norm_w': 1.0 + nrm(ks[1], (DEPTH, D_MODEL), 0.05),
        'w_in': nrm(ks[2], (DEPTH, D_MODEL, IN_WIDTH), D_MODEL ** -0.5),
        'hgrn_lower_bounds': nrm(ks[3], (DEPTH, HG_W), 0.5),
        'hgrn_onorm_w': 1.0 + nrm(ks[4], (DEPTH, HG_DV), 0.05),
        'w_hgrn_out': nrm(ks[5], (DEPTH, HG_VW, D_MODEL), HG_VW ** -0.5),
        'w_sb_out': nrm(ks[6], (DEPTH, SB_W, D_MODEL), SB_W ** -0.5),
        'diff_lambda': nrm(ks[7], (DEPTH, 4, DA_DH), 0.1),
        'diff_onorm_w': 1.0 + nrm(ks[8], (DEPTH, DA_DV), 0.05),
        'w_diff_out': nrm(ks[9], (DEPTH, DA_W, D_MODEL), DA_W ** -0.5),
        'rel_bias': nrm(ks[10], (REL_BUCKETS, DA_HEADS), 0.5),
        'w_out': nrm(ks[11], (DEPTH, D_MODEL, D_MODEL), D_MODEL ** -0.5),
        'ffn_norm_w': 1.0 + nrm(ks[12], (DEPTH, D_MODEL), 0.05),
        'w_up': nrm(ks[13], (DEPTH, D_MODEL, ff2), D_MODEL ** -0.5),
        'conv_w': nrm(ks[14], (DEPTH, CONV_W, ff2), CONV_W ** -0.5),
        'conv_b': nrm(ks[15], (DEPTH, ff2), 0.01),
        'w_down': nrm(ks[16], (DEPTH, D_FF, D_MODEL), D_FF ** -0.5),
        'final_norm_w': 1.0 + nrm(ks[17], (D_MODEL,), 0.05),
    }

def reference(x, attn_norm_w, w_in, hgrn_lower_bounds, hgrn_onorm_w, w_hgrn_out, w_sb_out,
              diff_lambda, diff_onorm_w, w_diff_out, rel_bias, w_out, ffn_norm_w, w_up,
              conv_w, conv_b, w_down, final_norm_w):
    lb_all = jnp.cumsum(jax.nn.softmax(hgrn_lower_bounds.astype(jnp.float32), axis=0), axis=0)
    lb_all = lb_all - lb_all[0]
    for l in range(DEPTH):
        h = _rmsnorm(x, attn_norm_w[l])
        (hq, hf, hi, hg, sq, sk, sv, dq, dk, dv, gate_logits) = _split_cols(h @ w_in[l])
        y_a = hgrn2_mixer(hq, hf, hi, hg, lb_all[l], hgrn_onorm_w[l]).astype(x.dtype) @ w_hgrn_out[l]
        y_b = stick_breaking_mixer(sq, sk, sv).astype(x.dtype) @ w_sb_out[l]
        y_c = diff_attention_mixer(dq, dk, dv, diff_lambda[l], diff_onorm_w[l], rel_bias,
                                   _lambda_init(l)).astype(x.dtype) @ w_diff_out[l]
        g_a, g_b, g_c = jnp.split(jax.nn.sigmoid(gate_logits), N_BRANCH, axis=-1)
        x = x + ((g_a * y_a + g_b * y_b + g_c * y_c) @ w_out[l]).astype(x.dtype)
        x = x + conv_glu_ffn(_rmsnorm(x, ffn_norm_w[l]), w_up[l], conv_w[l], conv_b[l],
                             w_down[l]).astype(x.dtype)
    return _rmsnorm(x, final_norm_w)


_drawn_inputs = setup_inputs


def setup_inputs(seed=0):
    import zlib

    import numpy as np

    out = dict(_drawn_inputs(seed))
    spreads = {}
    factors = {'hgrn_onorm_w': 3.697, 'conv_b': 8.0, 'diff_onorm_w': 3.813, 'ffn_norm_w': 3.15}
    for name, (base, spread) in spreads.items():
        noise = np.random.default_rng([zlib.crc32(name.encode()), seed]).standard_normal(out[name].shape)
        drawn = base * np.exp(spread * noise) if base else spread * noise
        out[name] = __import__('jax').numpy.asarray(drawn.astype(out[name].dtype))
    for name, factor in factors.items():
        out[name] = (out[name] * factor).astype(out[name].dtype)
    return out
```

```python
from contextlib import ExitStack, contextmanager
import math

import numpy as np
import concourse.bass as bass
from concourse import mybir

F32 = mybir.dt.float32
F32R = mybir.dt.float32r
I32 = mybir.dt.int32
ALU = mybir.AluOpType
ACT = mybir.ActivationFunctionType
AX = mybir.AxisListType

P = 128
S = 1024
D = 1024
KT = D // P
HALF = 512
NH = S // HALF
UNITS = 4
DH = 64
QK_SCALE = DH ** -0.5
HG_SCALE = P ** -0.5
NT = S // P
LEVELS = 7
FT = 2816 // P
BT = 512 // P
EPS = 1e-6
NEG = -1e30
EXP_CAP = 40.0
LAM_INIT = 0.8 - 0.6 * math.exp(0.0)
BUCKETS, MAX_DIST, DA_HEADS = 32, 128, 4
BIAS_COLS = P + S - 1
EXP_LN = "natural_log_exp_and_others"

HG_TILES = (0, 4, 8, 12)
SB_TILES = (16, 20, 24)
DA_TILES = (28, 32, 36)
GATE_TILE = (40, 48, 56)


def at_least(eng, sem, value):
    if not (isinstance(value, int) and value <= 0):
        eng.wait_ge(sem, value)


def is_first(u):
    return isinstance(u, int) and u == 0


def plain_wait(pool, opened):
    pool.sem_inc(opened, 1)


def f32(ap):
    return ap.bitcast(F32)


class Core:

    def __init__(self, nc, ctx):
        self.nc, self.ctx = nc, ctx
        self.hT_hi = self.sb("hT_hi", [P, KT, S], F32R)
        self.hT_lo = self.sb("hT_lo", [P, KT, S], F32R)
        self.R = self.sb("R", [P, KT, S], F32)
        self.ps = [ctx.enter_context(nc.psum_tensor(f"ps{i}", [P, S], F32)) for i in range(4)]
        self.ident = self.sb("ident", [P, P], F32)
        self.ones = self.sb("ones", [P, P], F32)
        self.eps = self.sb("eps", [P, 1], F32)
        self.normw = self.sb("normw", [P, 3, KT], F32)

    def sb(self, name, shape, dt, ctx=None):
        return (ctx or self.ctx).enter_context(self.nc.sbuf_tensor(name, shape, dt))

    def sems(self, names):
        made = [self.nc.alloc_semaphore(n) for n in names.split()]
        self.phase_sems += made
        return made

    @contextmanager
    def phase(self):
        self.phase_sems = []
        with ExitStack() as ctx:
            yield ctx
        self.nc.clear_and_free_semaphores(self.phase_sems)
        self.nc.all_engine_barrier()


def product(eng, out, a_hi, a_lo, b_hi, b_lo, start, stop):
    eng.matmul(out, a_hi, b_hi, start=start, stop=False, skip_group_check=True)
    eng.matmul(out, a_hi, b_lo, start=False, stop=False, skip_group_check=True)
    return eng.matmul(out, a_lo, b_hi, start=False, stop=stop, skip_group_check=True)


def setup_phase(core, consts, norm_w):
    nc = core.nc
    with core.phase() as ctx:
        const_in, pool_set = core.sems("const_in pool_set")
        block = ctx.enter_context(nc.Block())

        @block.sync
        def _(sp):
            sp.dma_start(core.ident[:], consts["ident"]).then_inc(const_in, 16)
            sp.dma_start(core.normw[:], norm_w).then_inc(const_in, 16)
            sp.wait_ge(const_in, 32)

        @block.gpsimd
        def _(pool):
            pool.memset(core.ones[:], 1.0)
            pool.memset(core.eps[:], EPS).then_inc(pool_set, 1)
            pool.wait_ge(pool_set, 1)


def norm_phase(core, tag, which, xT=None, out=None):
    nc = core.nc
    with core.phase() as ctx:
        sq_ready, sum_part, log_ready, rstd_ready, y_ready, hi_ready, lo_ready = core.sems(" ".join(f"{tag}_{n}" for n in
                          "sq_ready sum_part log_ready rstd_ready y_ready hi_ready lo_ready".split()))
        x_in = core.sems(" ".join(f"{tag}_x_in{kt}" for kt in range(KT if xT is not None else 0)))
        y_out = core.sems(" ".join(f"{tag}_y_out{i}" for i in range(2 if out is not None else 0)))
        sq = core.sb(f"{tag}_sq", [P, 2, S], F32, ctx)
        rstd = core.sb(f"{tag}_rstd", [P, S], F32, ctx)
        y = core.sb(f"{tag}_y", [P, 2, S], F32, ctx)
        total = core.ps[0]
        block = ctx.enter_context(nc.Block())

        @block.sync
        def _(sp):
            if xT is not None:
                for kt in range(KT):
                    sp.dma_start(core.R[:, kt], xT[:, kt]).then_inc(x_in[kt], 16)
            if out is not None:
                for kt in range(KT):
                    sp.wait_ge(y_ready, kt + 1)
                    sp.dma_start(out[:, kt], y[:, kt % 2]).then_inc(y_out[kt % 2], 16)
                for i in range(2):
                    sp.wait_ge(y_out[i], 16 * KT // 2)

        @block.scalar
        def _(act):
            act.preload_act_table_set(EXP_LN)
            for kt in range(KT):
                if xT is not None:
                    act.wait_ge(x_in[kt], 16)
                if kt >= 2:
                    act.wait_ge(sum_part, kt - 1)
                act.activation(sq[:, kt % 2], core.R[:, kt], ACT.Square).then_inc(sq_ready, 1)
            act.wait_ge(sum_part, KT)
            act.activation(rstd[:], total[:], ACT.Ln, bias=core.eps[:, 0:1],
                           scale=1.0 / D).then_inc(log_ready, 1)
            act.wait_ge(log_ready, 1)
            act.activation(rstd[:], rstd[:], ACT.Exp, scale=-0.5).then_inc(rstd_ready, 1)
            if out is None:
                for kt in range(KT):
                    act.wait_ge(y_ready, kt + 1)
                    act.activation(core.hT_hi[:, kt], y[:, kt % 2], ACT.Copy).then_inc(hi_ready, 1)

        @block.tensor
        def _(pe):
            for kt in range(KT):
                pe.wait_ge(sq_ready, kt + 1)
                for h in range(NH):
                    mm = pe.matmul(total[:, h * HALF:(h + 1) * HALF], core.ones[:],
                                   sq[:, kt % 2, h * HALF:(h + 1) * HALF],
                                   start=(kt == 0), stop=(kt == KT - 1))
                mm.then_inc(sum_part, 1)

        @block.vector
        def _(dve):
            dve.wait_ge(rstd_ready, 1)

            def lo_part(kt):
                dve.wait_ge(hi_ready, kt + 1)
                dve.tensor_tensor(core.hT_lo[:, kt], y[:, kt % 2], f32(core.hT_hi[:, kt]),
                                  ALU.subtract).then_inc(lo_ready, 1)

            for kt in range(KT):
                if out is not None and kt >= 2:
                    dve.wait_ge(y_out[kt % 2], 16 * (kt // 2))
                if out is None and kt >= 2:
                    dve.wait_ge(lo_ready, kt - 1)
                dve.scalar_tensor_tensor(out=y[:, kt % 2], in0=core.R[:, kt],
                                         scalar=core.normw[:, which, kt:kt + 1], in1=rstd[:],
                                         op0=ALU.mult, op1=ALU.mult).then_inc(y_ready, 1)
                if out is None and kt >= 1:
                    lo_part(kt - 1)
            if out is None:
                lo_part(KT - 1)


class WeightStream:

    def __init__(self, core, ctx, tag, per_unit, slots, raw_slots, kts=KT):
        assert per_unit % slots == 0 and per_unit % raw_slots == 0
        self.per_unit, self.kts, self.slots, self.raw_slots = per_unit, kts, slots, raw_slots
        self.raw = core.sb(f"{tag}_raw", [P, raw_slots, kts, P], F32, ctx)
        self.hi = core.sb(f"{tag}_hi", [P, slots, kts, P], F32R, ctx)
        self.lo = core.sb(f"{tag}_lo", [P, slots, kts, P], F32R, ctx)
        self.hi_made, self.split, self.open = core.sems(f"{tag}_hi_made {tag}_split {tag}_open")
        self.loaded = core.sems(" ".join(f"{tag}_loaded{i}" for i in range(raw_slots)))

    def load(self, sp, u, t, src):
        n = self.per_unit * u + t
        at_least(sp, self.split, n - self.raw_slots + 1)
        sp.dma_start(self.raw[:, t % self.raw_slots], src).then_inc(self.loaded[t % self.raw_slots], 16)

    def make(self, pool, u, t, read, reads):
        n, s, r = self.per_unit * u + t, t % self.slots, t % self.raw_slots
        loads = (self.per_unit // self.raw_slots) * u + t // self.raw_slots + 1
        raw = self.raw[:, r]
        pool.wait_ge(self.loaded[r], 16 * loads)
        at_least(pool, read, reads)
        plain_wait(pool, self.open)
        pool.tensor_scalar(self.hi[:, s], raw, 1.0, 0.0, ALU.mult, ALU.add).then_inc(self.hi_made, 1)
        pool.wait_ge(self.hi_made, n + 1)
        pool.tensor_tensor(self.lo[:, s], raw, f32(self.hi[:, s]), ALU.subtract).then_inc(self.split, 1)


class Projection:

    def __init__(self, core, ctx, tag, weights, ps, rhs):
        self.w, self.ps, self.rhs = weights, ps, rhs
        self.done, = core.sems(f"{tag}_done")
        self.free = core.sems(f"{tag}_free0 {tag}_free1")

    def bank(self, h):
        return self.ps[:, h * HALF:(h + 1) * HALF]

    def run(self, pe, u, t, free=None):
        rhs_hi, rhs_lo = self.rhs
        n, s = self.w.per_unit * u + t, t % self.w.slots
        free = free or [(self.free[h], n) for h in range(NH)]
        pe.wait_ge(self.w.split, n + 1)
        for h in range(NH):
            at_least(pe, *free[h])
            for kt in range(self.w.kts):
                mm = product(pe, self.bank(h), self.w.hi[:, s, kt], self.w.lo[:, s, kt],
                             rhs_hi[:, kt, h * HALF:(h + 1) * HALF], rhs_lo[:, kt, h * HALF:(h + 1) * HALF],
                             start=(kt == 0), stop=(kt == self.w.kts - 1))
            mm.then_inc(self.done, 1)

    def weights(self, pool, u, t):
        n = self.w.per_unit * u + t
        self.w.make(pool, u, t, self.done, NH * (n - self.w.slots + 1))



def merge_phase(core, b, w_in_t, w_branch_t, oT):
    nc = core.nc
    tag = f"m{b}"
    with core.phase() as ctx:
        o_hi = core.sb(f"{tag}_o_hi", [P, BT, S], F32R, ctx)
        o_lo = core.sb(f"{tag}_o_lo", [P, BT, S], F32R, ctx)
        sig = core.sb(f"{tag}_sig", [P, S], F32, ctx)
        part = core.sb(f"{tag}_part", [P, S], F32, ctx)
        WG = WeightStream(core, ctx, f"{tag}wg", 2, 2, 2)
        WY = WeightStream(core, ctx, f"{tag}wy", 2, 2, 2, kts=BT)
        gate = Projection(core, ctx, f"{tag}g", WG, core.ps[0], (core.hT_hi, core.hT_lo))
        y = Projection(core, ctx, f"{tag}y", WY, core.ps[1], (o_hi, o_lo))
        o_hi_ok, o_lo_ok, sig_ok, part_ok, sum_ok = core.sems(" ".join(f"{tag}_{n}" for n in "o_hi_ok o_lo_ok sig_ok part_ok sum_ok".split()))
        block = ctx.enter_context(nc.Block())

        @block.sync
        def _(sp):
            def unit(u):
                for t in range(2):
                    WG.load(sp, u, t, w_in_t[GATE_TILE[b] + 2 * u + t])
                    WY.load(sp, u, t, w_branch_t[b, 2 * u + t])

            unit(0)
            with sp.Fori(1, KT // 2) as u:
                unit(u)

        @block.gpsimd
        def _(pool):
            def unit(u):
                for t in range(2):
                    gate.weights(pool, u, t)
                    y.weights(pool, u, t)

            unit(0)
            with pool.Fori(1, KT // 2) as u:
                unit(u)

        @block.scalar
        def _(act):
            for k in range(BT):
                act.activation(o_hi[:, k], oT[:, k], ACT.Copy).then_inc(o_hi_ok, 1)

            def unit(u):
                for t in range(2):
                    for h in range(NH):
                        g = NH * (2 * u + t) + h
                        cols = slice(h * HALF, (h + 1) * HALF)
                        act.wait_ge(gate.done, g + 1)
                        at_least(act, part_ok, g - 1)
                        act.activation(sig[:, cols], gate.bank(h), ACT.Sigmoid).then_inc(sig_ok, 1)

            unit(0)
            with act.Fori(1, KT // 2) as u:
                unit(u)

        @block.vector
        def _(dve):
            for k in range(BT):
                dve.wait_ge(o_hi_ok, k + 1)
                dve.tensor_tensor(o_lo[:, k], oT[:, k], f32(o_hi[:, k]), ALU.subtract).then_inc(o_lo_ok, 1)

            def unit(u):
                for t in range(2):
                    for h in range(NH):
                        g = NH * (2 * u + t) + h
                        cols = slice(h * HALF, (h + 1) * HALF)
                        dve.wait_ge(sig_ok, g + 1)
                        dve.wait_ge(y.done, g + 1)
                        if b == 0:
                            dve.tensor_tensor(core.R[:, 2 * u + t, cols], y.bank(h), sig[:, cols],
                                              ALU.mult).then_inc(part_ok, 1)
                        else:
                            at_least(dve, sum_ok, g - 1)
                            dve.tensor_tensor(part[:, cols], y.bank(h), sig[:, cols], ALU.mult).then_inc(part_ok, 1)
                            dve.wait_ge(part_ok, g + 1)
                            dve.tensor_tensor(core.R[:, 2 * u + t, cols], part[:, cols], core.R[:, 2 * u + t, cols],
                                              ALU.add).then_inc(sum_ok, 1)

            unit(0)
            with dve.Fori(1, KT // 2) as u:
                unit(u)

        @block.tensor
        def _(pe):
            def unit(u):
                for t in range(2):
                    n = 2 * u + t
                    gate.run(pe, u, t, [(sig_ok, NH * n + h - 1) for h in range(NH)])
                    if isinstance(u, int) and t == 0:
                        pe.wait_ge(o_lo_ok, BT)
                    y.run(pe, u, t, [(part_ok, NH * n + h - 1) for h in range(NH)])

            unit(0)
            with pe.Fori(1, KT // 2) as u:
                unit(u)


def out_phase(core, w_out_t, xT):
    nc = core.nc
    with core.phase() as ctx:
        W = WeightStream(core, ctx, "ow", 2, 2, 2)
        proj = Projection(core, ctx, "op", W, core.ps[0], (core.hT_hi, core.hT_lo))
        hi_ok, lo_ok, sum_ok = core.sems("out_hi_ok out_lo_ok out_sum_ok")
        x_in = core.sems(" ".join(f"out_x_in{kt}" for kt in range(KT)))
        block = ctx.enter_context(nc.Block())

        @block.sync
        def _(sp):
            def unit(u):
                for t in range(2):
                    W.load(sp, u, t, w_out_t[2 * u + t])

            unit(0)
            for kt in range(KT):
                sp.wait_ge(lo_ok, kt + 1)
                sp.dma_start(core.R[:, kt], xT[:, kt]).then_inc(x_in[kt], 16)
            with sp.Fori(1, KT // 2) as u:
                unit(u)

        @block.gpsimd
        def _(pool):
            def unit(u):
                for t in range(2):
                    proj.weights(pool, u, t)

            unit(0)
            with pool.Fori(1, KT // 2) as u:
                unit(u)

        @block.scalar
        def _(act):
            for kt in range(KT):
                act.activation(core.hT_hi[:, kt], core.R[:, kt], ACT.Copy).then_inc(hi_ok, 1)

        @block.vector
        def _(dve):
            for kt in range(KT):
                dve.wait_ge(hi_ok, kt + 1)
                dve.tensor_tensor(core.hT_lo[:, kt], core.R[:, kt], f32(core.hT_hi[:, kt]),
                                  ALU.subtract).then_inc(lo_ok, 1)
            for kt in range(KT):
                dve.wait_ge(x_in[kt], 16)

            def unit(u):
                for t in range(2):
                    for h in range(NH):
                        cols = slice(h * HALF, (h + 1) * HALF)
                        dve.wait_ge(proj.done, NH * (2 * u + t) + h + 1)
                        dve.tensor_tensor(core.R[:, 2 * u + t, cols], proj.bank(h), core.R[:, 2 * u + t, cols],
                                          ALU.add).then_inc(proj.free[h], 1)

            unit(0)
            with dve.Fori(1, KT // 2) as u:
                unit(u)

        @block.tensor
        def _(pe):
            pe.wait_ge(lo_ok, KT)

            def unit(u):
                for t in range(2):
                    proj.run(pe, u, t)

            unit(0)
            with pe.Fori(1, KT // 2) as u:
                unit(u)



def mlp_phase(core, w_up_t, w_down_t, conv_in):
    nc = core.nc
    GROUPS = KT * NH
    UNITS_F = FT // 2
    with core.phase() as ctx:
        WU = WeightStream(core, ctx, "fu", 4, 2, 2)
        WD = WeightStream(core, ctx, "fd", 2, 2, 2)
        up = [Projection(core, ctx, f"f{n}", WU, core.ps[i], (core.hT_hi, core.hT_lo))
              for i, n in enumerate("gv")]
        conv_w = core.sb("f_conv_w", [P, 2 * FT, 4], F32, ctx)
        taps = core.sb("f_taps", [P, 2, 4], F32, ctx)
        c = core.sb("f_c", [P, 2, 2, S], F32, ctx)
        a_hi = core.sb("f_a_hi", [P, 2, S], F32R, ctx)
        a_lo = core.sb("f_a_lo", [P, 2, S], F32R, ctx)
        (conv_loaded, taps_ok, c0_ok, c1_ok, c2_ok, silu_ok, a_ok, a_hi_ok, a_lo_ok, down_ps, down_sum) = core.sems(" ".join("f_" + n for n in (
             "conv_loaded taps_ok c0_ok c1_ok c2_ok silu_ok a_ok a_hi_ok a_lo_ok down_ps down_sum").split()))
        block = ctx.enter_context(nc.Block())

        def down_bank(g):
            return core.ps[2 + g % 4 // 2][:, (g % 2) * HALF:(g % 2 + 1) * HALF]

        @block.sync
        def _(sp):
            sp.dma_start(conv_w[:], conv_in).then_inc(conv_loaded, 16)

            def unit(u):
                for t in range(2):
                    WU.load(sp, u, 2 * t, w_up_t[2 * u + t])
                    WU.load(sp, u, 2 * t + 1, w_up_t[2 * u + t + FT])
                for t in range(2):
                    WD.load(sp, u, t, w_down_t[2 * u + t])

            unit(0)
            with sp.Fori(1, UNITS_F) as u:
                unit(u)

        @block.gpsimd
        def _(pool):
            def unit(u):
                for t in range(2):
                    for i in range(2):
                        WU.make(pool, u, 2 * t + i, up[i].done, NH * (2 * u + t))
                for t in range(2):
                    WD.make(pool, u, t, down_ps, GROUPS * u)

            unit(0)
            with pool.Fori(1, UNITS_F) as u:
                unit(u)

        @block.scalar
        def _(act):
            def unit(u):
                for t in range(2):
                    f = 2 * u + t
                    for i in range(2):
                        n = 2 * f + i
                        act.wait_ge(up[i].done, NH * (f + 1))
                        act.wait_ge(taps_ok, n + 1)
                        at_least(act, a_lo_ok, f - 1)
                        act.activation(c[:, t, i], core.ps[i][:], ACT.Identity, bias=taps[:, i, 3:4],
                                       scale=taps[:, i, 2:3]).then_inc(c0_ok, 1)
                        if i == 0:
                            act.wait_ge(c2_ok, n + 1)
                            act.activation(c[:, t, 0], c[:, t, 0], ACT.Silu).then_inc(silu_ok, 1)
                    act.wait_ge(a_ok, f + 1)
                    at_least(act, down_ps, GROUPS * u)
                    act.activation(a_hi[:, t], c[:, t, 0], ACT.Copy).then_inc(a_hi_ok, 1)

            unit(0)
            with act.Fori(1, UNITS_F) as u:
                unit(u)

        def sum_down(dve, u):
            for g in range(GROUPS):
                d, h = g // NH, g % NH
                cols = slice(h * HALF, (h + 1) * HALF)
                dve.wait_ge(down_ps, GROUPS * u + g + 1)
                dve.tensor_tensor(core.R[:, d, cols], down_bank(g), core.R[:, d, cols], ALU.add).then_inc(down_sum, 1)

        @block.vector
        def _(dve):
            dve.wait_ge(conv_loaded, 16)

            def unit(u):
                for t in range(2):
                    f = 2 * u + t
                    for i in range(2):
                        n = 2 * f + i
                        at_least(dve, c2_ok, n - 1)
                        dve.tensor_copy(taps[:, i], conv_w[:, f + FT * i]).then_inc(taps_ok, 1)
                    for i in range(2):
                        n = 2 * f + i
                        dve.wait_ge(c0_ok, n + 1)
                        for lag, done in ((1, c1_ok), (2, c2_ok)):
                            if lag == 2:
                                dve.wait_ge(c1_ok, n + 1)
                            dve.scalar_tensor_tensor(out=c[:, t, i, lag:S], in0=core.ps[i][:, 0:S - lag],
                                                     scalar=taps[:, i, 2 - lag:3 - lag], in1=c[:, t, i, lag:S],
                                                     op0=ALU.mult, op1=ALU.add).then_inc(done, 1)
                    if t == 0 and not is_first(u):
                        sum_down(dve, u - 1)
                    dve.wait_ge(silu_ok, f + 1)
                    dve.wait_ge(c2_ok, 2 * f + 2)
                    dve.tensor_tensor(c[:, t, 0], c[:, t, 0], c[:, t, 1], ALU.mult).then_inc(a_ok, 1)
                    dve.wait_ge(a_hi_ok, f + 1)
                    dve.tensor_tensor(a_lo[:, t], c[:, t, 0], f32(a_hi[:, t]), ALU.subtract).then_inc(a_lo_ok, 1)

            unit(0)
            with dve.Fori(1, UNITS_F) as u:
                unit(u)
            sum_down(dve, UNITS_F - 1)

        @block.tensor
        def _(pe):
            def down(u):
                pe.wait_ge(a_lo_ok, 2 * (u + 1))
                pe.wait_ge(WD.split, 2 * (u + 1))
                for g in range(GROUPS):
                    d, h = g // NH, g % NH
                    cols = slice(h * HALF, (h + 1) * HALF)
                    at_least(pe, down_sum, GROUPS * u + g - 3)
                    for t in range(2):
                        mm = product(pe, down_bank(g), WD.hi[:, t, d], WD.lo[:, t, d], a_hi[:, t, cols],
                                     a_lo[:, t, cols], t == 0, t == 1)
                    mm.then_inc(down_ps, 1)

            def unit(u):
                for t in range(2):
                    f = 2 * u + t
                    for i in range(2):
                        up[i].run(pe, u, 2 * t + i, [(c2_ok, 2 * (f - 1) + i + 1)] * NH)
                    if t == 0 and not is_first(u):
                        down(u - 1)

            unit(0)
            unit(1)
            with pe.Fori(2, UNITS_F) as u:
                unit(u)
            down(UNITS_F - 1)



SB_STEPS = [(c, j, h) for c in range(NH) for j in range(4 * c + 3, -1, -1) for h in range(2)]


def sb_columns(c, j):
    t0 = max(HALF * c, P * j)
    return t0, HALF * (c + 1) - t0


def stick_breaking_phase(core, w_in_t, consts, small, oT):
    nc = core.nc
    NZ, NE, NS, NW = 3, 2, 3, 2
    with core.phase() as ctx:
        W = WeightStream(core, ctx, "sbw", 3, 3, 1)
        proj = Projection(core, ctx, "sbp", W, core.ps[3], (core.hT_hi, core.hT_lo))
        (masks_in, q_hi_ok, q_lo_ok, vT_ok, v_turned, v_hi_ok, v_lo_ok, pads_ok,
         z_ok, zc_ok, cap_ok, e_ok, l_ok, sp_ok, sp_hi_ok, sp_lo_ok, tri_ok, arg_ok, rest_ok,
         w_ok, w_hi_ok, w_lo_ok, pv_ok, o_read) = core.sems(" ".join("sb_" + n for n in (
                "masks_in q_hi_ok q_lo_ok vT_ok v_turned v_hi_ok v_lo_ok pads_ok z_ok zc_ok cap_ok e_ok l_ok "
                "sp_ok sp_hi_ok sp_lo_ok tri_ok arg_ok rest_ok w_ok w_hi_ok w_lo_ok pv_ok o_read").split()))
        qk_hi = core.sb("sb_qk_hi", [P, 2, S], F32R, ctx)
        qk_lo = core.sb("sb_qk_lo", [P, 2, S], F32R, ctx)
        v_hi = core.sb("sb_v_hi", [P, NT, 3, DH], F32R, ctx)
        v_lo = core.sb("sb_v_lo", [P, NT, 3, DH], F32R, ctx)
        zc = core.sb("sb_zc", [P, NZ, HALF], F32, ctx)
        e = core.sb("sb_e", [P, NE, HALF], F32, ctx)
        sp_hi = core.sb("sb_sp_hi", [P, NS, HALF], F32R, ctx)
        sp_lo = core.sb("sb_sp_lo", [P, NS, HALF], F32R, ctx)
        w = core.sb("sb_w", [P, NW, HALF], F32, ctx)
        w_hi = core.sb("sb_w_hi", [P, NW, HALF], F32R, ctx)
        w_lo = core.sb("sb_w_lo", [P, NW, HALF], F32R, ctx)
        mask_raw = core.sb("sb_mask_raw", [P, 4, P], F32, ctx)
        mask = core.sb("sb_mask", [P, 4, P], F32R, ctx)
        vT = zc[:].rearrange("p a b -> p (a b)")[:, 0:S]
        z_ps, c_ps, o_ps = core.ps[0], core.ps[1], core.ps[2]
        K = len(SB_STEPS)
        block = ctx.enter_context(nc.Block())

        @block.sync
        def _(sp):
            sp.dma_start(mask_raw[:], consts["sb_masks"]).then_inc(masks_in, 16)

            def unit(u):
                for t, first in enumerate(SB_TILES):
                    W.load(sp, u, t, w_in_t[first + u])

            unit(0)
            with sp.Fori(1, UNITS) as u:
                unit(u)

        @block.gpsimd
        def _(pool):
            pool.memset(f32(v_hi[:, :, 1]), 0.0)
            pool.memset(f32(v_lo[:, :, 1]), 0.0).then_inc(pads_ok, 1)
            pool.wait_ge(masks_in, 16)
            pool.tensor_scalar(mask[:], mask_raw[:], 1.0, 0.0, ALU.mult, ALU.add).then_inc(pads_ok, 1)

            def unit(u):
                for t in range(3):
                    proj.weights(pool, u, t)
                for k in range(K + 3):
                    if k >= 3:
                        m = k - 3
                        n = sb_columns(*SB_STEPS[m][:2])[1]
                        pool.wait_ge(w_ok, K * u + m + 1)
                        at_least(pool, pv_ok, K * u + m - NW + 1)
                        plain_wait(pool, W.open)
                        pool.tensor_scalar(w_hi[:, m % NW, 0:n], w[:, m % NW, 0:n], 1.0, 0.0,
                                           ALU.mult, ALU.add).then_inc(w_hi_ok, 1)
                    if k < K:
                        n = sb_columns(*SB_STEPS[k][:2])[1]
                        pool.wait_ge(sp_ok, K * u + k + 1)
                        at_least(pool, rest_ok, K * u + k - NS + 1)
                        plain_wait(pool, W.open)
                        pool.tensor_scalar(sp_hi[:, k % NS, 0:n], e[:, k % NE, 0:n], 1.0, 0.0,
                                           ALU.mult, ALU.add).then_inc(sp_hi_ok, 1)
                        pool.wait_ge(sp_hi_ok, K * u + k + 1)
                        pool.tensor_tensor(sp_lo[:, k % NS, 0:n], e[:, k % NE, 0:n],
                                           f32(sp_hi[:, k % NS, 0:n]), ALU.subtract).then_inc(sp_lo_ok, 1)

            unit(0)
            with pool.Fori(1, UNITS) as u:
                unit(u)

        @block.scalar
        def _(act):
            act.preload_act_table_set(EXP_LN)
            def unit(u):
                for t in range(2):
                    for h in range(NH):
                        act.wait_ge(proj.done, NH * (3 * u + t) + h + 1)
                        at_least(act, z_ok, K * u)
                        act.activation(qk_hi[:, t, h * HALF:(h + 1) * HALF], proj.bank(h), ACT.Copy,
                                       scale=QK_SCALE if t == 0 else 1.0).then_inc(q_hi_ok, 1)
                for h in range(NH):
                    act.wait_ge(proj.done, NH * (3 * u + 2) + h + 1)
                    at_least(act, arg_ok, K * u)
                    act.activation(vT[:, h * HALF:(h + 1) * HALF], proj.bank(h),
                                   ACT.Copy).then_inc(proj.free[h], 1)
                for h in range(NH):
                    act.wait_ge(v_turned, NH * u + h + 1)
                    at_least(act, pv_ok, K * u)
                    act.activation(v_hi[:, 4 * h:4 * h + 4, 0:3:2, :],
                                   z_ps[:, h * HALF:(h + 1) * HALF].rearrange("p (a b c) -> p a b c", a=4, b=2),
                                   ACT.Copy).then_inc(v_hi_ok, 1)
                act.wait_ge(v_lo_ok, NH * (u + 1))
                for k in range(K + 2):
                    if k < K:
                        n = sb_columns(*SB_STEPS[k][:2])[1]
                        act.wait_ge(z_ok, K * u + k + 1)
                        at_least(act, arg_ok, K * u + k - NZ + 1)
                        act.activation(zc[:, k % NZ, 0:n], z_ps[:, (k % 2) * HALF:(k % 2) * HALF + n],
                                       ACT.Copy).then_inc(zc_ok, 1)
                    if k >= 2:
                        m = k - 2
                        n = sb_columns(*SB_STEPS[m][:2])[1]
                        act.wait_ge(arg_ok, K * u + m + 1)
                        act.activation(w[:, m % NW, 0:n], w[:, m % NW, 0:n], ACT.Exp).then_inc(w_ok, 1)
                    if k < K:
                        n = sb_columns(*SB_STEPS[k][:2])[1]
                        act.wait_ge(cap_ok, K * u + k + 1)
                        act.activation(e[:, k % NE, 0:n], e[:, k % NE, 0:n], ACT.Exp).then_inc(e_ok, 1)
                        act.wait_ge(e_ok, K * u + k + 1)
                        act.activation(e[:, k % NE, 0:n], e[:, k % NE, 0:n], ACT.Ln,
                                       bias=1.0).then_inc(l_ok, 1)
                    if k == SB_STEPS.index((1, 6, 0)):
                        act.wait_ge(pv_ok, K * u + 8)
                        act.activation(oT[:, u, 0:HALF], o_ps[:, 0:HALF], ACT.Copy).then_inc(o_read, 1)
                act.wait_ge(pv_ok, K * (u + 1))
                act.activation(oT[:, u, HALF:S], o_ps[:, HALF:S], ACT.Copy).then_inc(o_read, 1)

            unit(0)
            with act.Fori(1, UNITS) as u:
                unit(u)

        @block.vector
        def _(dve):
            def unit(u):
                for t in range(2):
                    for h in range(NH):
                        cols = slice(h * HALF, (h + 1) * HALF)
                        dve.wait_ge(q_hi_ok, 2 * NH * u + NH * t + h + 1)
                        dve.scalar_tensor_tensor(out=qk_lo[:, t, cols], in0=proj.bank(h),
                                                 scalar=QK_SCALE if t == 0 else 1.0,
                                                 in1=f32(qk_hi[:, t, cols]), op0=ALU.mult,
                                                 op1=ALU.subtract).then_inc(proj.free[h], 1)
                for h in range(NH):
                    dve.wait_ge(v_hi_ok, NH * u + h + 1)
                    dve.tensor_tensor(v_lo[:, 4 * h:4 * h + 4, 0:3:2, :],
                                      z_ps[:, h * HALF:(h + 1) * HALF].rearrange("p (a b c) -> p a b c", a=4, b=2),
                                      f32(v_hi[:, 4 * h:4 * h + 4, 0:3:2, :]), ALU.subtract).then_inc(v_lo_ok, 1)
                for k in range(K + 3):
                    if k < K:
                        n = sb_columns(*SB_STEPS[k][:2])[1]
                        dve.wait_ge(zc_ok, K * u + k + 1)
                        at_least(dve, sp_lo_ok, K * u + k - NE + 1)
                        dve.tensor_scalar(e[:, k % NE, 0:n], zc[:, k % NZ, 0:n], EXP_CAP, None,
                                          ALU.min).then_inc(cap_ok, 1)
                    if 2 <= k < K + 2:
                        m = k - 2
                        c, j, h = SB_STEPS[m]
                        t0, n = sb_columns(c, j)
                        dve.wait_ge(tri_ok, K * u + m + 1)
                        at_least(dve, w_lo_ok, K * u + m - NW + 1)
                        dve.tensor_tensor(w[:, m % NW, 0:n], zc[:, m % NZ, 0:n],
                                          c_ps[:, h * HALF + HALF - n:(h + 1) * HALF],
                                          ALU.subtract).then_inc(arg_ok, 1)
                    if k >= 3:
                        m = k - 3
                        n = sb_columns(*SB_STEPS[m][:2])[1]
                        dve.wait_ge(w_hi_ok, K * u + m + 1)
                        at_least(dve, pv_ok, K * u + m - NW + 1)
                        dve.tensor_tensor(w_lo[:, m % NW, 0:n], w[:, m % NW, 0:n],
                                          f32(w_hi[:, m % NW, 0:n]), ALU.subtract).then_inc(w_lo_ok, 1)
                    if k < K:
                        n = sb_columns(*SB_STEPS[k][:2])[1]
                        dve.wait_ge(l_ok, K * u + k + 1)
                        dve.tensor_tensor(e[:, k % NE, 0:n], e[:, k % NE, 0:n], zc[:, k % NZ, 0:n],
                                          ALU.max).then_inc(sp_ok, 1)

            unit(0)
            with dve.Fori(1, UNITS) as u:
                unit(u)

        @block.tensor
        def _(pe):
            def unit(u):
                for t in range(3):
                    proj.run(pe, u, t)
                for h in range(NH):
                    pe.wait_ge(proj.free[h], 3 * u + 3)
                    for a in range(4):
                        col = h * HALF + a * P
                        mm = pe.transpose(z_ps[:, col:col + P], vT[:, col:col + P], core.ident[:])
                    mm.then_inc(v_turned, 1)
                if isinstance(u, int):
                    pe.wait_ge(pads_ok, 2)
                pe.wait_ge(v_lo_ok, NH * (u + 1))
                for k in range(K + 4):
                    if k < K:
                        c, j, h = SB_STEPS[k]
                        t0, n = sb_columns(c, j)
                        rows, bank = slice(DH * h, DH * (h + 1)), (k % 2) * HALF
                        at_least(pe, zc_ok, K * u + k - 1)
                        mm = product(pe, z_ps[:, bank:bank + n],
                                     qk_hi[rows, 1, P * j:P * (j + 1)], qk_lo[rows, 1, P * j:P * (j + 1)],
                                     qk_hi[rows, 0, t0:t0 + n], qk_lo[rows, 0, t0:t0 + n], True, j < 4 * c)
                        if j >= 4 * c:
                            mm = pe.matmul(z_ps[:, bank:bank + P], mask[:, 0], mask[:, 3],
                                           start=False, stop=True, skip_group_check=True)
                        mm.then_inc(z_ok, 1)
                    if k >= 3 and k - 3 < K:
                        m = k - 3
                        c, j, h = SB_STEPS[m]
                        n = sb_columns(c, j)[1]
                        pe.wait_ge(arg_ok, K * u + m + 1)
                        for part in (sp_hi, sp_lo):
                            mm = pe.matmul(c_ps[:, (h + 1) * HALF - n:(h + 1) * HALF], mask[:, 2],
                                           part[:, m % NS, 0:n], start=False, stop=(j == 0),
                                           skip_group_check=True)
                        mm.then_inc(rest_ok, 1)
                    if k >= 1 and k - 1 < K:
                        m = k - 1
                        c, j, h = SB_STEPS[m]
                        n = sb_columns(c, j)[1]
                        pe.wait_ge(sp_lo_ok, K * u + m + 1)
                        for part in (sp_hi, sp_lo):
                            mm = pe.matmul(c_ps[:, (h + 1) * HALF - n:(h + 1) * HALF], mask[:, 1],
                                           part[:, m % NS, 0:n],
                                           start=(j == 4 * c + 3 and part is sp_hi), stop=False,
                                           skip_group_check=True)
                        mm.then_inc(tri_ok, 1)
                    if k >= 4:
                        m = k - 4
                        c, j, h = SB_STEPS[m]
                        t0, n = sb_columns(c, j)
                        if m == 0 or m == 8:
                            at_least(pe, o_read, NH * u + c - 1)
                        pe.wait_ge(w_lo_ok, K * u + m + 1)
                        mm = product(pe, o_ps[:, t0:t0 + n], v_hi[:, j, h:h + 2], v_lo[:, j, h:h + 2],
                                     w_hi[:, m % NW, 0:n], w_lo[:, m % NW, 0:n],
                                     (j == 4 * c + 3 and h == 0), (j == 0 and h == 1))
                        mm.then_inc(pv_ok, 1)

            unit(0)
            with pe.Fori(1, UNITS) as u:
                unit(u)



def turn_v(pe, free_sem, free_value, vT, ps, ident, turned):
    for h in range(NH):
        pe.wait_ge(free_sem[h], free_value)
        for a in range(4):
            col = h * HALF + a * P
            mm = pe.transpose(ps[:, col:col + P], vT[:, col:col + P], ident)
        mm.then_inc(turned, 1)



HG_PARTS = ("f", "q", "v", "g")


def hgrn2_phase(core, w_in_t, consts, small, oT):
    nc = core.nc
    F, Q, V, G = range(4)
    with core.phase() as ctx:
        W = WeightStream(core, ctx, "hgw", 4, 2, 2)
        proj = Projection(core, ctx, "hgp", W, core.ps[3], (core.hT_hi, core.hT_lo))
        names = ("small_in zf_ok nab_ok ez_ok lz_ok logf_ok cum_ok sp_ok key_ok q_ok vT_ok v_turned v_hi_ok "
                 "v_lo_ok gz_ok gn_ok ge_ok gl_ok ga_ok gs_ok silu_ok last_ok kd_d kd_e kd_ok kd_turned kdT_hi_ok "
                 "kdT_lo_ok upd_ok el_ok state_ok state_hi_ok state_lo_ok lev_d lev_e lev_x lev_hi lev_lo lev_ps "
                 "score_ok s_hi_ok s_lo_ok qe_e qe_ok qe_hi_ok qe_lo_ok out_ps sq_ok ss_ok ln_ok rstd_ok rg_ok o_ok "
                 "score_zero").split()
        sem = dict(zip(names, core.sems(" ".join("hg_" + n for n in names))))
        zf, e, cum, key, q, gz = (core.R[:, i] for i in range(6))
        x = core.R[:, 6:8]
        vT = e
        score = core.sb("hg_score", [P, NT, P], F32, ctx)
        state = core.sb("hg_state", [P, NT, P], F32, ctx)
        elast = core.sb("hg_elast", [P, NT], F32, ctx)
        levels = core.sb("hg_levels", [P, LEVELS + 1, P], I32, ctx)
        onorm = core.sb("hg_onorm", [P, 1], F32, ctx)
        v_hi, v_lo = (core.sb(f"hg_v_{p}", [P, NT, P], F32R, ctx) for p in ("hi", "lo"))
        pair_hi, pair_lo = (core.sb(f"hg_pair_{p}", [P, 3, S], F32R, ctx) for p in ("hi", "lo"))
        t_ps, k_ps, o_ps = core.ps[0], core.ps[1], core.ps[2]
        chunks = lambda ap: ap.rearrange("p (c t) -> p c t", t=P)
        L1 = LEVELS + 1
        block = ctx.enter_context(nc.Block())

        def halves(ap, l):
            return ap.rearrange("p (b two t) -> p b two t", two=2, t=P >> (l + 1))

        @block.sync
        def _(sp):
            sp.dma_start(levels[:], consts["hg_levels"]).then_inc(sem["small_in"], 16)
            sp.dma_start(onorm[:], small["hg_onorm"]).then_inc(sem["small_in"], 16)

            def unit(u):
                for t, part in enumerate((HG_TILES[1], HG_TILES[0], HG_TILES[2], HG_TILES[3])):
                    W.load(sp, u, t, w_in_t[part + u])

            unit(0)
            with sp.Fori(1, UNITS) as u:
                unit(u)

        @block.gpsimd
        def _(pool):
            pool.memset(score[:], 0.0)
            pool.memset(state[:, 0], 0.0).then_inc(sem["score_zero"], 1)

            def unit(u):
                for t in range(4):
                    proj.weights(pool, u, t)
                for l in range(LEVELS):
                    pool.wait_ge(sem["lev_hi"], (LEVELS + 2) * u + l + 1)
                    pool.tensor_tensor(pair_lo[:, l % 2], x[:, l % 2], f32(pair_hi[:, l % 2]),
                                       ALU.subtract).then_inc(sem["lev_lo"], 1)

            unit(0)
            with pool.Fori(1, UNITS) as u:
                unit(u)

        @block.scalar
        def _(act):
            act.preload_act_table_set(EXP_LN)

            def copy_half(u, t, h, dst, scale=1.0):
                act.wait_ge(proj.done, NH * (4 * u + t) + h + 1)
                act.activation(dst[:, h * HALF:(h + 1) * HALF], proj.bank(h), ACT.Copy,
                               scale=scale).then_inc(proj.free[h], 1)

            def step(name, value, out, in_, func, **kw):
                act.activation(out, in_, func, **kw).then_inc(sem[name], 1)

            def unit(u):
                at_least(act, sem["o_ok"], NH * u)
                for h in range(NH):
                    copy_half(u, F, h, zf)
                for h in range(NH):
                    copy_half(u, Q, h, q, HG_SCALE)
                act.wait_ge(proj.free[1], 4 * u + 1)
                act.activation(e, zf, ACT.Abs).then_inc(sem["nab_ok"], 1)
                act.wait_ge(sem["nab_ok"], u + 1)
                act.activation(e, e, ACT.Exp, scale=-1.0).then_inc(sem["ez_ok"], 1)
                act.wait_ge(sem["ez_ok"], u + 1)
                act.activation(e, e, ACT.Ln, bias=1.0).then_inc(sem["lz_ok"], 1)
                act.wait_ge(sem["sp_ok"], u + 1)
                act.activation(key, e, ACT.Exp, scale=-1.0).then_inc(sem["key_ok"], 1)
                act.wait_ge(sem["key_ok"], u + 1)
                for h in range(NH):
                    copy_half(u, V, h, vT)
                act.wait_ge(sem["cum_ok"], NT * (u + 1))
                act.activation(elast[:], chunks(cum)[:, :, P - 1], ACT.Exp).then_inc(sem["el_ok"], 1)
                act.wait_ge(sem["kd_d"], u + 1)
                act.activation(x[:, 0], x[:, 0], ACT.Exp).then_inc(sem["kd_e"], 1)
                for h in range(NH):
                    cols = slice(h * HALF, (h + 1) * HALF)
                    act.wait_ge(sem["v_turned"], NH * u + h + 1)
                    act.activation(v_hi[:, 4 * h:4 * h + 4], chunks(t_ps[:, cols]), ACT.Copy).then_inc(sem["v_hi_ok"], 1)
                act.wait_ge(sem["kd_turned"], u + 1)
                act.activation(pair_hi[:, 0], k_ps[:], ACT.Copy).then_inc(sem["kdT_hi_ok"], 1)
                act.wait_ge(sem["state_ok"], (NT - 1) * (u + 1))
                act.activation(pair_hi[:, 2], state[:].rearrange("p c t -> p (c t)"),
                               ACT.Copy).then_inc(sem["state_hi_ok"], 1)
                for h in range(NH):
                    copy_half(u, G, h, gz)
                for l in range(LEVELS + 1):
                    if l < LEVELS:
                        act.wait_ge(sem["lev_d"], LEVELS * u + l + 1)
                        d = halves(x[:, l % 2], l)
                        act.activation(d[:, :, 0], d[:, :, 0], ACT.Exp, scale=-1.0)
                        act.activation(d[:, :, 1], d[:, :, 1], ACT.Exp).then_inc(sem["lev_e"], 1)
                    if l >= 1:
                        m = l - 1
                        act.wait_ge(sem["lev_x"], LEVELS * u + m + 1)
                        if m < 2:
                            act.wait_ge(sem["upd_ok"], u + 1)
                        else:
                            act.wait_ge(sem["lev_ps"], L1 * u + m - 1)
                        act.activation(pair_hi[:, m % 2], x[:, m % 2], ACT.Copy).then_inc(sem["lev_hi"], 1)
                act.wait_ge(sem["lev_ps"], L1 * u + LEVELS - 1)
                act.activation(pair_hi[:, 1], key, ACT.Copy).then_inc(sem["lev_hi"], 1)
                act.wait_ge(sem["lev_ps"], L1 * u + LEVELS)
                act.activation(pair_hi[:, 0], q, ACT.Copy).then_inc(sem["lev_hi"], 1)
                act.wait_ge(sem["lev_lo"], LEVELS * (u + 1))
                act.activation(x[:, 1], cum, ACT.Exp).then_inc(sem["qe_e"], 1)
                act.wait_ge(sem["sp_ok"], u + 1)
                act.activation(zf, gz, ACT.Abs).then_inc(sem["gn_ok"], 1)
                act.wait_ge(sem["gn_ok"], u + 1)
                act.activation(zf, zf, ACT.Exp, scale=-1.0).then_inc(sem["ge_ok"], 1)
                act.wait_ge(sem["ge_ok"], u + 1)
                act.activation(zf, zf, ACT.Ln, bias=1.0).then_inc(sem["gl_ok"], 1)
                act.wait_ge(sem["ga_ok"], u + 1)
                act.activation(zf, zf, ACT.Exp).then_inc(sem["gs_ok"], 1)
                act.wait_ge(sem["qe_ok"], u + 1)
                act.wait_ge(sem["lev_ps"], L1 * (u + 1))
                act.activation(pair_hi[:, 1], x[:, 1], ACT.Copy).then_inc(sem["qe_hi_ok"], 1)
                act.wait_ge(sem["score_ok"], L1 * (u + 1))
                act.activation(pair_hi[:, 0], score[:].rearrange("p c t -> p (c t)"),
                               ACT.Copy).then_inc(sem["s_hi_ok"], 1)
                for h in range(NH):
                    cols = slice(h * HALF, (h + 1) * HALF)
                    act.wait_ge(sem["out_ps"], NH * u + h + 1)
                    act.activation(x[:, 0, cols], o_ps[:, cols], ACT.Square).then_inc(sem["sq_ok"], 1)
                for h in range(NH):
                    cols = slice(h * HALF, (h + 1) * HALF)
                    act.wait_ge(sem["ss_ok"], NH * u + h + 1)
                    act.wait_ge(sem["qe_lo_ok"], u + 1)
                    act.activation(x[:, 1, cols], t_ps[:, cols], ACT.Ln, bias=core.eps[:, 0:1],
                                   scale=1.0 / P).then_inc(sem["ln_ok"], 1)
                    act.wait_ge(sem["ln_ok"], NH * u + h + 1)
                    act.activation(x[:, 1, cols], x[:, 1, cols], ACT.Exp, scale=-0.5).then_inc(sem["rstd_ok"], 1)

            unit(0)
            with act.Fori(1, UNITS) as u:
                unit(u)

        @block.vector
        def _(dve):
            dve.wait_ge(sem["small_in"], 32)
            dve.wait_ge(sem["score_zero"], 1)

            def unit(u):
                dve.wait_ge(sem["lz_ok"], u + 1)
                dve.scalar_tensor_tensor(out=x[:, 1], in0=zf, scalar=0.0, in1=e, op0=ALU.min,
                                         op1=ALU.subtract).then_inc(sem["logf_ok"], 1)
                dve.wait_ge(sem["logf_ok"], u + 1)
                dve.scalar_tensor_tensor(out=e, in0=zf, scalar=0.0, in1=e, op0=ALU.max,
                                         op1=ALU.add).then_inc(sem["sp_ok"], 1)
                for c in range(NT):
                    cols = slice(P * c, P * (c + 1))
                    dve.tensor_tensor_scan(cum[:, cols], core.ones[:], x[:, 1, cols], 0.0, ALU.mult,
                                           ALU.add).then_inc(sem["cum_ok"], 1)
                dve.wait_ge(sem["cum_ok"], NT * (u + 1))
                dve.tensor_tensor(chunks(x[:, 0]), chunks(cum)[:, :, P - 1:P].to_broadcast([P, NT, P]), chunks(cum),
                                  ALU.subtract).then_inc(sem["kd_d"], 1)
                dve.wait_ge(sem["kd_e"], u + 1)
                dve.wait_ge(sem["key_ok"], u + 1)
                dve.tensor_tensor(x[:, 0], x[:, 0], key, ALU.mult).then_inc(sem["kd_ok"], 1)
                for h in range(NH):
                    cols = slice(h * HALF, (h + 1) * HALF)
                    dve.wait_ge(sem["v_hi_ok"], NH * u + h + 1)
                    dve.tensor_tensor(v_lo[:, 4 * h:4 * h + 4], chunks(t_ps[:, cols]),
                                      f32(v_hi[:, 4 * h:4 * h + 4]), ALU.subtract).then_inc(sem["v_lo_ok"], 1)
                dve.wait_ge(sem["kdT_hi_ok"], u + 1)
                dve.tensor_tensor(pair_lo[:, 0], k_ps[:], f32(pair_hi[:, 0]), ALU.subtract).then_inc(sem["kdT_lo_ok"], 1)
                dve.wait_ge(sem["upd_ok"], u + 1)
                dve.wait_ge(sem["el_ok"], u + 1)
                at_least(dve, sem["state_lo_ok"], u)
                for c in range(NT - 1):
                    at_least(dve, sem["state_ok"], (NT - 1) * u + c)
                    dve.scalar_tensor_tensor(out=state[:, c + 1], in0=state[:, c], scalar=elast[:, c:c + 1],
                                             in1=o_ps[:, P * c:P * (c + 1)], op0=ALU.mult,
                                             op1=ALU.add).then_inc(sem["state_ok"], 1)
                dve.wait_ge(sem["state_hi_ok"], u + 1)
                dve.tensor_tensor(pair_lo[:, 2], state[:].rearrange("p c t -> p (c t)"), f32(pair_hi[:, 2]),
                                  ALU.subtract).then_inc(sem["state_lo_ok"], 1)

                def keep(l):
                    dve.wait_ge(sem["lev_ps"], L1 * u + l + 1)
                    at_least(dve, sem["score_ok"], L1 * u + l)
                    dve.sem_inc(sem["small_in"], 1)
                    dve.copy_predicated(score[:], levels[:, l:l + 1].to_broadcast([P, NT, P]),
                                        chunks((t_ps, k_ps)[l % 2][:])).then_inc(sem["score_ok"], 1)

                for l in range(LEVELS + 1):
                    if l < LEVELS:
                        h = P >> (l + 1)
                        blocks = lambda ap: ap.rearrange("p (b t) -> p b t", t=2 * h)
                        if l >= 2:
                            dve.wait_ge(sem["lev_lo"], LEVELS * u + l - 1)
                        else:
                            dve.wait_ge(sem["kd_turned"], u + 1)
                        dve.tensor_tensor(blocks(x[:, l % 2]), blocks(cum),
                                          blocks(cum)[:, :, h - 1:h].to_broadcast([P, S // (2 * h), 2 * h]),
                                          ALU.subtract).then_inc(sem["lev_d"], 1)
                    if l >= 2:
                        keep(l - 2)
                    if l < LEVELS:
                        dve.wait_ge(sem["lev_e"], LEVELS * u + l + 1)
                        if l == 0:
                            dve.wait_ge(proj.free[1], 4 * u + 2)
                        d = halves(x[:, l % 2], l)
                        dve.tensor_tensor(d[:, :, 0], d[:, :, 0], halves(key, l)[:, :, 0], ALU.mult)
                        dve.tensor_tensor(d[:, :, 1], d[:, :, 1], halves(q, l)[:, :, 1],
                                          ALU.mult).then_inc(sem["lev_x"], 1)
                keep(LEVELS - 1)
                dve.wait_ge(sem["lev_hi"], (LEVELS + 2) * u + LEVELS + 1)
                dve.tensor_tensor(pair_lo[:, 1], key, f32(pair_hi[:, 1]), ALU.subtract)
                dve.wait_ge(sem["lev_hi"], (LEVELS + 2) * (u + 1))
                dve.tensor_tensor(pair_lo[:, 0], q, f32(pair_hi[:, 0]), ALU.subtract).then_inc(sem["last_ok"], 1)
                dve.wait_ge(sem["qe_e"], u + 1)
                dve.tensor_tensor(x[:, 1], x[:, 1], q, ALU.mult).then_inc(sem["qe_ok"], 1)
                dve.wait_ge(sem["gl_ok"], u + 1)
                dve.scalar_tensor_tensor(out=zf, in0=gz, scalar=0.0, in1=zf, op0=ALU.min,
                                         op1=ALU.subtract).then_inc(sem["ga_ok"], 1)
                dve.wait_ge(sem["gs_ok"], u + 1)
                dve.tensor_tensor(gz, gz, zf, ALU.mult).then_inc(sem["silu_ok"], 1)
                keep(LEVELS)
                dve.wait_ge(sem["qe_hi_ok"], u + 1)
                dve.tensor_tensor(pair_lo[:, 1], x[:, 1], f32(pair_hi[:, 1]), ALU.subtract).then_inc(sem["qe_lo_ok"], 1)
                dve.wait_ge(sem["s_hi_ok"], u + 1)
                dve.tensor_tensor(pair_lo[:, 0], score[:].rearrange("p c t -> p (c t)"), f32(pair_hi[:, 0]),
                                  ALU.subtract).then_inc(sem["s_lo_ok"], 1)
                for h in range(NH):
                    cols = slice(h * HALF, (h + 1) * HALF)
                    dve.wait_ge(sem["rstd_ok"], NH * u + h + 1)
                    if h == 0:
                        dve.wait_ge(sem["silu_ok"], u + 1)
                    dve.tensor_tensor(x[:, 1, cols], x[:, 1, cols], gz[:, cols], ALU.mult).then_inc(sem["rg_ok"], 1)
                    dve.wait_ge(sem["rg_ok"], NH * u + h + 1)
                    dve.scalar_tensor_tensor(out=oT[:, u, cols], in0=o_ps[:, cols], scalar=onorm[:, 0:1],
                                             in1=x[:, 1, cols], op0=ALU.mult, op1=ALU.mult).then_inc(sem["o_ok"], 1)

            unit(0)
            with dve.Fori(1, UNITS) as u:
                unit(u)

        @block.tensor
        def _(pe):
            def unit(u):
                for t in range(3):
                    proj.run(pe, u, t)
                at_least(pe, sem["rstd_ok"], NH * u)
                turn_v(pe, proj.free, 4 * u + 3, vT, t_ps, core.ident[:], sem["v_turned"])
                pe.wait_ge(sem["kd_ok"], u + 1)
                for c in range(NT):
                    mm = pe.transpose(k_ps[:, P * c:P * (c + 1)], x[:, 0, P * c:P * (c + 1)], core.ident[:])
                mm.then_inc(sem["kd_turned"], 1)
                proj.run(pe, u, 3)
                pe.wait_ge(sem["v_lo_ok"], NH * (u + 1))
                pe.wait_ge(sem["kdT_lo_ok"], u + 1)
                at_least(pe, sem["o_ok"], NH * u)
                for c in range(NT - 1):
                    cols = slice(P * c, P * (c + 1))
                    mm = product(pe, o_ps[:, cols], pair_hi[:, 0, cols], pair_lo[:, 0, cols], v_hi[:, c], v_lo[:, c],
                                 True, True)
                mm.then_inc(sem["upd_ok"], 1)
                for l in range(LEVELS + 1):
                    a = b = l % 2
                    if l < LEVELS:
                        pe.wait_ge(sem["lev_lo"], LEVELS * u + l + 1)
                    else:
                        a, b = 1, 0
                        pe.wait_ge(sem["last_ok"], u + 1)
                    at_least(pe, sem["score_ok"], L1 * u + l - 1)
                    for c in range(NT):
                        cols = slice(P * c, P * (c + 1))
                        mm = product(pe, (t_ps, k_ps)[l % 2][:, cols], pair_hi[:, a, cols], pair_lo[:, a, cols],
                                     pair_hi[:, b, cols], pair_lo[:, b, cols], True, True)
                    mm.then_inc(sem["lev_ps"], 1)
                pe.wait_ge(sem["state_lo_ok"], u + 1)
                pe.wait_ge(sem["qe_lo_ok"], u + 1)
                pe.wait_ge(sem["s_lo_ok"], u + 1)
                for c in range(NT):
                    cols = slice(P * c, P * (c + 1))
                    mm = product(pe, o_ps[:, cols], v_hi[:, c], v_lo[:, c], pair_hi[:, 0, cols], pair_lo[:, 0, cols],
                                 True, c == 0)
                    if c:
                        mm = product(pe, o_ps[:, cols], pair_hi[:, 2, cols], pair_lo[:, 2, cols],
                                     pair_hi[:, 1, cols], pair_lo[:, 1, cols], False, True)
                    if c % 4 == 3:
                        mm.then_inc(sem["out_ps"], 1)
                for h in range(NH):
                    cols = slice(h * HALF, (h + 1) * HALF)
                    pe.wait_ge(sem["sq_ok"], NH * u + h + 1)
                    pe.matmul(t_ps[:, cols], core.ones[:], x[:, 0, cols], start=True, stop=True).then_inc(sem["ss_ok"], 1)

            unit(0)
            with pe.Fori(1, UNITS) as u:
                unit(u)



def differential_phase(core, w_in_t, consts, small, oT):
    nc = core.nc
    with core.phase() as ctx:
        W = WeightStream(core, ctx, "daw", 3, 3, 1)
        proj = Projection(core, ctx, "dap", W, core.ps[3], (core.hT_hi, core.hT_lo))
        (small_in, row_ok, row_sum, row_out, flip_ok, bias_ok, lam_step, bias_in, qk_hi_ok, v_turned, v_hi_ok, v_lo_ok,
         lg_ps_ok, lg_ok, nm_ok, p_ok, comb_step, w_ok, turned_ok, wT_hi_ok, wT_lo_ok, pv_ok, sq_ok, ss_ok,
         ln_ok, rstd_ok, o_ok, dve_open) = core.sems(" ".join("da_" + n for n in (
             "small_in row_ok row_sum row_out flip_ok bias_ok lam_step bias_in qk_hi_ok v_turned v_hi_ok v_lo_ok lg_ps_ok lg_ok "
             "nm_ok p_ok comb_step w_ok turned_ok wT_hi_ok wT_lo_ok pv_ok sq_ok ss_ok ln_ok rstd_ok o_ok "
             "dve_open").split()))
        qk_hi = core.sb("da_qk_hi", [P, 2, S], F32R, ctx)
        qk_lo = core.sb("da_qk_lo", [P, 2, S], F32R, ctx)
        v_hi = core.sb("da_v_hi", [P, NT, P], F32R, ctx)
        v_lo = core.sb("da_v_lo", [P, NT, P], F32R, ctx)
        lg = core.sb("da_lg", [P, 2, 2, S], F32, ctx)
        wT_hi = core.sb("da_wT_hi", [P, S], F32R, ctx)
        wT_lo = core.sb("da_wT_lo", [P, S], F32R, ctx)
        bias = core.sb("da_bias", [P, S], F32, ctx)
        mx = core.sb("da_mx", [P, 2, 2], F32, ctx)
        nm = core.sb("da_nm", [P, 2, 2], F32, ctx)
        sm = core.sb("da_sm", [P, 2, 2], F32, ctx)
        rs = core.sb("da_rs", [P, 2, 2], F32, ctx)
        rl = core.sb("da_rl", [P, 2], F32, ctx)
        lam4 = core.sb("da_lam4", [P, 4, DH], F32, ctx)
        lam2 = core.sb("da_lam2", [P, 2], F32, ctx)
        neg_lam = core.sb("da_neg_lam", [P, 1], F32, ctx)
        onorm = core.sb("da_onorm", [P, 1], F32, ctx)
        vT = lg[:, 0, 0]
        sq, rstd = lg[:, 0, 0], lg[:, 0, 1]
        table = lg[0:BUCKETS, 1, 0, 0:DA_HEADS]
        row_mask = lg[0:DA_HEADS, 0].rearrange("p m s -> p (m s)")[:, 0:BIAS_COLS]
        hot = core.sb("da_hot", [BUCKETS, BIAS_COLS], F32, ctx)
        row_dram = nc.dram_tensor("da_bias_rows", [DA_HEADS, BIAS_COLS], F32).ap()
        flip = core.sb("da_flip", [P, P], F32, ctx)
        hankel = lg[:, 1, 1]
        t_ps, o_ps = core.ps[2], core.ps[3]
        block = ctx.enter_context(nc.Block())

        @block.sync
        def _(sp):
            for dst, src in ((hot[:], consts["da_hot"]), (table, small["rel_bias"]), (row_mask, consts["da_row_mask"]),
                             (lam4[:], small["lam"].partition_broadcast(P)), (onorm[:], small["da_onorm"]), (flip[:], consts["flip"])):
                sp.dma_start(dst, src).then_inc(small_in, 16)
            sp.wait_ge(row_sum, 3)
            sp.dma_start(row_dram, row_mask).then_inc(row_out, 16)
            sp.wait_ge(row_out, 16)

            def unit(u):
                for t, first in enumerate(DA_TILES):
                    W.load(sp, u, t, w_in_t[first + u])
                at_least(sp, o_ok, NH * u)
                src = row_dram[u, 0:S]
                src = bass.AP(src.tensor, src.offset, [[1, P], [1, S]])
                sp.dma_start(hankel, src).then_inc(bias_in, 16)

            unit(0)
            with sp.Fori(1, UNITS) as u:
                unit(u)

        @block.gpsimd
        def _(pool):
            def unit(u):
                for t in range(3):
                    proj.weights(pool, u, t)

            unit(0)
            with pool.Fori(1, UNITS) as u:
                unit(u)

        @block.scalar
        def _(act):
            act.preload_act_table_set(EXP_LN)
            act.wait_ge(lam_step, 2)
            act.activation(lam2[:], lam2[:], ACT.Exp).then_inc(lam_step, 1)

            def unit(u):
                for t in range(2):
                    for h in range(NH):
                        act.wait_ge(proj.done, NH * (3 * u + t) + h + 1)
                        act.activation(qk_hi[:, t, h * HALF:(h + 1) * HALF], proj.bank(h), ACT.Copy,
                                       scale=QK_SCALE if t == 0 else 1.0).then_inc(qk_hi_ok, 1)
                if isinstance(u, int):
                    act.wait_ge(row_out, 16)
                else:
                    act.wait_ge(o_ok, NH * u)
                for h in range(NH):
                    act.wait_ge(proj.done, NH * (3 * u + 2) + h + 1)
                    act.activation(vT[:, h * HALF:(h + 1) * HALF], proj.bank(h),
                                   ACT.Copy).then_inc(proj.free[h], 1)
                act.wait_ge(flip_ok, u + 1)
                act.activation(bias[:], core.ps[0][:], ACT.Copy).then_inc(bias_ok, 1)
                for h in range(NH):
                    act.wait_ge(v_turned, NH * u + h + 1)
                    act.activation(v_hi[:, 4 * h:4 * h + 4, :],
                                   t_ps[:, h * HALF:(h + 1) * HALF].rearrange("p (a b) -> p a b", a=4),
                                   ACT.Copy).then_inc(v_hi_ok, 1)
                for i in range(NT + 1):
                    if i < NT:
                        n = P * (i + 1)
                        act.wait_ge(nm_ok, NT * u + i + 1)
                        for m in range(2):
                            x = lg[:, i % 2, m, 0:n]
                            act.activation(x, x, ACT.Exp, bias=nm[:, i % 2, m:m + 1],
                                           accum_out=sm[:, i % 2, m:m + 1]).then_inc(p_ok, 1)
                    if i >= 1:
                        n = P * i
                        act.wait_ge(turned_ok, NT * u + i)
                        at_least(act, pv_ok, NT * u + i - 1)
                        act.activation(wT_hi[:, 0:n], t_ps[:, 0:n], ACT.Copy).then_inc(wT_hi_ok, 1)
                for h in range(NH):
                    cols = slice(h * HALF, (h + 1) * HALF)
                    act.wait_ge(pv_ok, NT * (u + 1))
                    act.activation(sq[:, cols], o_ps[:, cols], ACT.Square).then_inc(sq_ok, 1)
                for h in range(NH):
                    cols = slice(h * HALF, (h + 1) * HALF)
                    act.wait_ge(ss_ok, NH * u + h + 1)
                    act.activation(rstd[:, cols], t_ps[:, cols], ACT.Ln, bias=core.eps[:, 0:1],
                                   scale=1.0 / P).then_inc(ln_ok, 1)
                    act.wait_ge(ln_ok, NH * u + h + 1)
                    act.activation(rstd[:, cols], rstd[:, cols], ACT.Exp, scale=-0.5).then_inc(rstd_ok, 1)

            unit(0)
            with act.Fori(1, UNITS) as u:
                unit(u)

        @block.vector
        def _(dve):
            dve.wait_ge(small_in, 16 * 6)
            dve.tensor_tensor(lam4[:, 0:4:2], lam4[:, 0:4:2], lam4[:, 1:4:2], ALU.mult).then_inc(lam_step, 1)
            dve.wait_ge(lam_step, 1)
            dve.tensor_reduce(lam2[:], lam4[:, 0:4:2], AX.X, ALU.add).then_inc(lam_step, 1)
            dve.tensor_scalar(onorm[:], onorm[:], 1.0 - LAM_INIT, None, ALU.mult).then_inc(comb_step, 1)
            dve.wait_ge(lam_step, 3)
            dve.tensor_tensor(neg_lam[:], lam2[:, 1:2], lam2[:, 0:1], ALU.subtract).then_inc(lam_step, 1)
            dve.wait_ge(lam_step, 4)
            dve.tensor_scalar(neg_lam[:], neg_lam[:], -LAM_INIT, None, ALU.add).then_inc(lam_step, 1)
            for b, (lo, hi) in enumerate(bias_chunks()):
                dve.wait_ge(row_ok, 3)
                dve.tensor_tensor(row_mask[:, lo:hi], bias_bank(core, b)[0:DA_HEADS, 0:hi - lo], row_mask[:, lo:hi],
                                  ALU.add).then_inc(row_sum, 1)

            def unit(u):
                for t in range(2):
                    for h in range(NH):
                        cols = slice(h * HALF, (h + 1) * HALF)
                        dve.wait_ge(qk_hi_ok, 2 * NH * u + NH * t + h + 1)
                        dve.scalar_tensor_tensor(out=qk_lo[:, t, cols], in0=proj.bank(h),
                                                 scalar=QK_SCALE if t == 0 else 1.0,
                                                 in1=f32(qk_hi[:, t, cols]), op0=ALU.mult,
                                                 op1=ALU.subtract).then_inc(proj.free[h], 1)
                for h in range(NH):
                    dve.wait_ge(v_hi_ok, NH * u + h + 1)
                    dve.tensor_tensor(v_lo[:, 4 * h:4 * h + 4, :],
                                      t_ps[:, h * HALF:(h + 1) * HALF].rearrange("p (a b) -> p a b", a=4),
                                      f32(v_hi[:, 4 * h:4 * h + 4, :]), ALU.subtract).then_inc(v_lo_ok, 1)
                dve.wait_ge(bias_ok, u + 1)
                for i in range(NT + 2):
                    if i < NT:
                        n, s = P * (i + 1), i % 2
                        for m in range(2):
                            dve.wait_ge(lg_ps_ok, 2 * (NT * u + i) + m + 1)
                            if i >= 2:
                                dve.wait_ge(turned_ok, NT * u + i - 1)
                            dve.sem_inc(dve_open, 1)
                            dve.tensor_tensor_reduce(lg[:, s, m, 0:n], core.ps[m][:, 0:n], bias[:, S - n:S],
                                                     1.0, 3 * NEG, ALU.add, ALU.max,
                                                     mx[:, s, m:m + 1]).then_inc(lg_ok, 1)
                        dve.wait_ge(lg_ok, 2 * (NT * u + i + 1))
                        dve.tensor_scalar(nm[:, s], mx[:, s], -1.0, None, ALU.mult).then_inc(nm_ok, 1)
                    if i >= 2:
                        n = P * (i - 1)
                        dve.wait_ge(wT_hi_ok, NT * u + i - 1)
                        dve.tensor_tensor(wT_lo[:, 0:n], t_ps[:, 0:n], f32(wT_hi[:, 0:n]),
                                          ALU.subtract).then_inc(wT_lo_ok, 1)
                    if 1 <= i <= NT:
                        n, s, g = P * i, (i - 1) % 2, NT * u + i
                        dve.wait_ge(p_ok, 2 * g)
                        dve.reciprocal(rs[:, s], sm[:, s]).then_inc(comb_step, 1)
                        dve.wait_ge(comb_step, 3 * g - 1)
                        dve.tensor_tensor(rl[:, s:s + 1], rs[:, s, 1:2], neg_lam[:], ALU.mult).then_inc(comb_step, 1)
                        dve.tensor_scalar(lg[:, s, 0, 0:n], lg[:, s, 0, 0:n], rs[:, s, 0:1], None,
                                          ALU.mult).then_inc(comb_step, 1)
                        dve.wait_ge(comb_step, 3 * g + 1)
                        dve.scalar_tensor_tensor(out=lg[:, s, 0, 0:n], in0=lg[:, s, 1, 0:n], scalar=rl[:, s:s + 1],
                                                 in1=lg[:, s, 0, 0:n], op0=ALU.mult, op1=ALU.add).then_inc(w_ok, 1)
                for h in range(NH):
                    cols = slice(h * HALF, (h + 1) * HALF)
                    dve.wait_ge(rstd_ok, NH * u + h + 1)
                    dve.scalar_tensor_tensor(out=oT[:, u, cols], in0=o_ps[:, cols], scalar=onorm[:, 0:1],
                                             in1=rstd[:, cols], op0=ALU.mult, op1=ALU.mult).then_inc(o_ok, 1)

            unit(0)
            with dve.Fori(1, UNITS) as u:
                unit(u)

        @block.tensor
        def _(pe):
            pe.wait_ge(small_in, 16 * 6)
            for b, (lo, hi) in enumerate(bias_chunks()):
                pe.matmul(bias_bank(core, b)[0:DA_HEADS, 0:hi - lo], table, hot[:, lo:hi],
                          start=True, stop=True).then_inc(row_ok, 1)

            def logits(u, i):
                for m in range(2):
                    at_least(pe, lg_ok, 2 * (NT * u + i - 1) + m + 1)
                    rows, n = slice(DH * m, DH * (m + 1)), P * (i + 1)
                    for lo in range(0, n, HALF):
                        hi = min(n, lo + HALF)
                        mm = product(pe, core.ps[m][:, lo:hi],
                                     qk_hi[rows, 0, P * i:P * (i + 1)], qk_lo[rows, 0, P * i:P * (i + 1)],
                                     qk_hi[rows, 1, lo:hi], qk_lo[rows, 1, lo:hi], True, True)
                    mm.then_inc(lg_ps_ok, 1)

            def unit(u):
                at_least(pe, o_ok, NH * u)
                for t in range(3):
                    proj.run(pe, u, t)
                turn_v(pe, proj.free, 3 * u + 3, vT, t_ps, core.ident[:], v_turned)
                pe.wait_ge(bias_in, 16 * (u + 1))
                if isinstance(u, int):
                    pe.wait_ge(row_sum, 3)
                for h in range(NH):
                    cols = slice(h * HALF, (h + 1) * HALF)
                    mm = pe.matmul(core.ps[0][:, cols], flip[:], hankel[:, cols], start=True, stop=True)
                mm.then_inc(flip_ok, 1)
                pe.wait_ge(bias_ok, u + 1)
                pe.wait_ge(v_lo_ok, NH * (u + 1))
                logits(u, 0)
                for i in range(NT + 1):
                    if i + 1 < NT:
                        logits(u, i + 1)
                    if i >= 1:
                        pe.wait_ge(wT_lo_ok, NT * u + i)
                        for j in range(i):
                            cols = slice(P * j, P * (j + 1))
                            mm = product(pe, o_ps[:, P * (i - 1):P * i], v_hi[:, j], v_lo[:, j],
                                         wT_hi[:, cols], wT_lo[:, cols], j == 0, j == i - 1)
                        mm.then_inc(pv_ok, 1)
                    if i < NT:
                        pe.wait_ge(w_ok, NT * u + i + 1)
                        for j in range(i + 1):
                            mm = pe.transpose(t_ps[:, P * j:P * (j + 1)], lg[:, i % 2, 0, P * j:P * (j + 1)],
                                              core.ident[:])
                        mm.then_inc(turned_ok, 1)
                for h in range(NH):
                    pe.wait_ge(sq_ok, NH * u + h + 1)
                    pe.matmul(t_ps[:, h * HALF:(h + 1) * HALF], core.ones[:], sq[:, h * HALF:(h + 1) * HALF],
                              start=True, stop=True).then_inc(ss_ok, 1)

            unit(0)
            with pe.Fori(1, UNITS) as u:
                unit(u)


def bias_chunks():
    return [(lo, min(BIAS_COLS, lo + HALF)) for lo in range(0, BIAS_COLS, HALF)]


def bias_bank(core, b):
    return core.ps[b // 2][:, (b % 2) * HALF:(b % 2 + 1) * HALF]


def dump_phase(core, src, out):
    nc = core.nc
    with core.phase() as ctx:
        dumped, = core.sems("dumped")
        block = ctx.enter_context(nc.Block())

        @block.sync
        def _(sp):
            sp.dma_start(out, src).then_inc(dumped, 16)
            sp.wait_ge(dumped, 16)


OUT_SHAPE = (P, KT, S)
FULL = True


def program(nc, dram, out):
    with ExitStack() as ctx:
        core = Core(nc, ctx)
        setup_phase(core, dram, dram["norm_w"])
        norm_phase(core, "n1", 0, xT=dram["xT"])
        with ExitStack() as attention:
            oT = core.sb("oT", [P, BT, S], F32, attention)
            for b, branch in enumerate((hgrn2_phase, stick_breaking_phase, differential_phase)):
                branch(core, dram["w_in_t"], dram, dram, oT)
                merge_phase(core, b, dram["w_in_t"], dram["w_branch_t"], oT)
        out_phase(core, dram["w_out_t"], dram["xT"])
        norm_phase(core, "n2", 1)
        mlp_phase(core, dram["w_up_t"], dram["w_down_t"], dram["conv"])
        norm_phase(core, "n3", 2, out=out)


def host_constants():
    i = np.arange(P)
    key, query = i[:, None], i[None, :]
    eye = np.eye(P, dtype=np.float32)
    later = (key >= query).astype(np.float32)
    sb = np.stack([eye, later, 1 - later, np.where(key >= query, NEG, 0)], axis=1).astype(np.float32)
    dist = np.arange(S - 1, -P, -1)
    n = np.maximum(dist, 0)
    exact = BUCKETS // 2
    scaled = np.log(np.maximum(n, 1).astype(np.float32) / exact) / math.log(MAX_DIST / exact)
    large = np.minimum(exact + (scaled * (BUCKETS - exact)).astype(np.int32), BUCKETS - 1)
    bucket = np.where(n < exact, n, large)
    hot = (np.arange(BUCKETS)[:, None] == bucket[None, :]).astype(np.float32)
    row_mask = np.broadcast_to(np.where(dist < 0, NEG, 0).astype(np.float32), (DA_HEADS, BIAS_COLS))
    level = np.zeros((P, LEVELS + 1, P), np.int32)
    for l in range(LEVELS):
        h = P >> (l + 1)
        level[:, l] = (key // (2 * h) == query // (2 * h)) & (key % (2 * h) < h) & (query % (2 * h) >= h)
    level[:, LEVELS] = key == query
    return {"ident": eye, "flip": np.ascontiguousarray(eye[::-1]), "sb_masks": np.ascontiguousarray(sb), "da_hot": hot,
            "da_row_mask": np.ascontiguousarray(row_mask), "hg_levels": level}


def col_tiles(w, np_=np):
    r, c = w.shape
    return np.ascontiguousarray(w.reshape(r // P, P, c // P, P).transpose(2, 1, 0, 3))


def kernel(**inputs):
    import concourse.bacc as bacc
    from concourse.bass_utils import run_bass_kernel_spmd as run
    a = {k: np.asarray(v) for k, v in inputs.items()}
    nc = bacc.Bacc("TRN2", target_bir_lowering=False, num_devices=1)
    feature_major = lambda x: np.ascontiguousarray(x.T.reshape(KT, P, S).transpose(1, 0, 2))
    arrays = {
        "xT": feature_major(a["x"][0]),
        "w_in_t": col_tiles(a["w_in"][0]),
        "norm_w": np.ascontiguousarray(np.stack([a["attn_norm_w"][0], a["ffn_norm_w"][0], a["final_norm_w"]])
                                       .reshape(3, KT, P).transpose(2, 0, 1)),
        "w_branch_t": np.stack([col_tiles(a[n][0]) for n in ("w_hgrn_out", "w_sb_out", "w_diff_out")]),
        "w_out_t": col_tiles(a["w_out"][0]),
        "w_up_t": col_tiles(a["w_up"][0]),
        "w_down_t": np.ascontiguousarray(a["w_down"][0].reshape(FT, P, KT, P)),
        "conv": np.ascontiguousarray(np.concatenate([a["conv_w"][0], a["conv_b"]])
                                     .reshape(4, 2 * FT, P).transpose(2, 1, 0)),
        "rel_bias": a["rel_bias"],
        "lam": a["diff_lambda"][0],
        "da_onorm": np.ascontiguousarray(a["diff_onorm_w"].T),
        "hg_onorm": np.ascontiguousarray(a["hgrn_onorm_w"].T),
        **host_constants(),
    }
    dram = {n: nc.dram_tensor("in_" + n, v.shape, mybir.dt.from_np(v.dtype), kind="ExternalInput").ap()
            for n, v in arrays.items()}
    out = nc.dram_tensor("out0", OUT_SHAPE, F32, kind="ExternalOutput").ap()
    program(nc, dram, out)
    rows = lambda y: np.ascontiguousarray(y.transpose(1, 0, 2).reshape(D, S).T)[None] if FULL else y
    r = run(nc, [{"in_" + n: v for n, v in arrays.items()}], core_ids=[0])
    return rows(r.results[0]["out0"])
```

```python
from contextlib import ExitStack, contextmanager
import math

import numpy as np
import concourse.bass as bass
from concourse import mybir

F32 = mybir.dt.float32
F32R = mybir.dt.float32r
I32 = mybir.dt.int32
ALU = mybir.AluOpType
ACT = mybir.ActivationFunctionType
AX = mybir.AxisListType

P = 128
S = 1024
D = 1024
KT = D // P
HALF = 512
NH = S // HALF
UNITS = 4
DH = 64
QK_SCALE = DH ** -0.5
HG_SCALE = P ** -0.5
NT = S // P
LEVELS = 7
FT = 2816 // P
BT = 512 // P
EPS = 1e-6
NEG = -1e30
EXP_CAP = 40.0
LAM_INIT = 0.8 - 0.6 * math.exp(0.0)
BUCKETS, MAX_DIST, DA_HEADS = 32, 128, 4
BIAS_COLS = P + S - 1
EXP_LN = "natural_log_exp_and_others"

HG_TILES = (0, 4, 8, 12)
SB_TILES = (16, 20, 24)
DA_TILES = (28, 32, 36)
GATE_TILE = (40, 48, 56)
EARLY_GATES = (4, 3, 3)


def at_least(eng, sem, value):
    if not (isinstance(value, int) and value <= 0):
        eng.wait_ge(sem, value)


def is_first(u):
    return isinstance(u, int) and u == 0


def is_gates(u):
    return isinstance(u, int) and u == UNITS


def plain_wait(pool, opened):
    pool.sem_inc(opened, 1)


def f32(ap):
    return ap.bitcast(F32)


class Core:

    def __init__(self, nc, ctx):
        self.nc, self.ctx = nc, ctx
        self.hT_hi = self.sb("hT_hi", [P, KT, S], F32R)
        self.hT_lo = self.sb("hT_lo", [P, KT, S], F32R)
        self.ps = [ctx.enter_context(nc.psum_tensor(f"ps{i}", [P, S], F32)) for i in range(4)]
        self.ident = self.sb("ident", [P, P], F32)
        self.ones = self.sb("ones", [P, P], F32)
        self.eps = self.sb("eps", [P, 1], F32)
        self.normw = self.sb("normw", [P, 3, KT], F32)

    def sb(self, name, shape, dt, ctx=None):
        return (ctx or self.ctx).enter_context(self.nc.sbuf_tensor(name, shape, dt))

    def sems(self, names):
        made = [self.nc.alloc_semaphore(n) for n in names.split()]
        self.phase_sems += made
        return made

    @contextmanager
    def phase(self):
        self.phase_sems = []
        with ExitStack() as ctx:
            yield ctx
        self.nc.clear_and_free_semaphores(self.phase_sems)
        self.nc.all_engine_barrier()


def product(eng, out, a_hi, a_lo, b_hi, b_lo, start, stop):
    eng.matmul(out, a_hi, b_hi, start=start, stop=False, skip_group_check=True)
    eng.matmul(out, a_hi, b_lo, start=False, stop=False, skip_group_check=True)
    return eng.matmul(out, a_lo, b_hi, start=False, stop=stop, skip_group_check=True)


class Rms:

    def __init__(self, core, tag, source, sq, acc, total, rstd):
        self.core, self.source, self.sq, self.acc, self.total, self.rstd = core, source, sq, acc, total, rstd
        self.sq_ready, self.added, self.summed, self.log_ready, self.ready = core.sems(" ".join(
            f"{tag}_{n}" for n in "sq_ready added summed log_ready rstd_ready".split()))

    def square(self, act, kt):
        if kt >= 2:
            act.wait_ge(self.added, max(1, kt - 2))
        act.activation(self.sq[kt % 2], self.source(kt), ACT.Square).then_inc(self.sq_ready, 1)

    def add(self, dve, kt):
        if kt == 0:
            return
        dve.wait_ge(self.sq_ready, kt + 1)
        if kt >= 2:
            dve.wait_ge(self.added, kt - 1)
        dve.tensor_tensor(self.acc, self.sq[0] if kt == 1 else self.acc, self.sq[kt % 2],
                          ALU.add).then_inc(self.added, 1)

    def sum(self, pe):
        pe.wait_ge(self.added, KT - 1)
        for h in range(NH):
            cols = slice(h * HALF, (h + 1) * HALF)
            mm = pe.matmul(self.total[:, cols], self.core.ones[:], self.acc[:, cols], start=True, stop=True)
        mm.then_inc(self.summed, 1)

    def root(self, act):
        act.wait_ge(self.summed, 1)
        act.activation(self.rstd, self.total[:], ACT.Ln, bias=self.core.eps[:, 0:1],
                       scale=1.0 / D).then_inc(self.log_ready, 1)
        act.wait_ge(self.log_ready, 1)
        act.activation(self.rstd, self.rstd, ACT.Exp, scale=-0.5).then_inc(self.ready, 1)


class Features:
    ON_POOL = (3, 5, 7)

    def __init__(self, core, tag, source):
        self.core, self.source = core, source
        self.hi_ok, self.lo_dve, self.lo_pool = core.sems(f"{tag}_hi_ok {tag}_lo_dve {tag}_lo_pool")

    def hi(self, act, kt):
        act.activation(self.core.hT_hi[:, kt], self.source(kt), ACT.Copy).then_inc(self.hi_ok, 1)

    def lo(self, eng, kt, done):
        eng.wait_ge(self.hi_ok, kt + 1)
        eng.tensor_tensor(self.core.hT_lo[:, kt], self.source(kt), f32(self.core.hT_hi[:, kt]),
                          ALU.subtract).then_inc(done, 1)

    def on_pool(self, pool):
        for kt in self.ON_POOL:
            self.lo(pool, kt, self.lo_pool)

    def on_dve(self, dve, kt):
        if kt not in self.ON_POOL:
            self.lo(dve, kt, self.lo_dve)

    def wait(self, eng, kt):
        pools = sum(k <= kt for k in self.ON_POOL)
        if kt in self.ON_POOL:
            eng.wait_ge(self.lo_pool, pools)
        else:
            eng.wait_ge(self.lo_dve, kt + 1 - pools)


class Normalize:
    SLOTS = 3

    def __init__(self, core, tag, which, source, rstd, y):
        self.core, self.which, self.source, self.rstd, self.y = core, which, source, rstd, y
        self.y_ready, = core.sems(f"{tag}_y_ready")
        self.features = Features(core, tag, lambda kt: y[kt % self.SLOTS])

    def on_dve(self, dve):
        for kt in range(KT):
            if kt >= self.SLOTS:
                self.features.wait(dve, kt - self.SLOTS)
            dve.scalar_tensor_tensor(out=self.y[kt % self.SLOTS], in0=self.source(kt),
                                     scalar=self.core.normw[:, self.which, kt:kt + 1], in1=self.rstd,
                                     op0=ALU.mult, op1=ALU.mult).then_inc(self.y_ready, 1)
            if kt:
                self.features.on_dve(dve, kt - 1)
        self.features.on_dve(dve, KT - 1)

    def on_act(self, act):
        for kt in range(KT):
            act.wait_ge(self.y_ready, kt + 1)
            self.features.hi(act, kt)


class WeightStream:

    def __init__(self, core, ctx, tag, per_unit, slots, raw_slots, kts=KT, pieces=1):
        assert per_unit % slots == 0 and per_unit % raw_slots == 0
        self.per_unit, self.kts, self.slots, self.raw_slots = per_unit, kts, slots, raw_slots
        self.pieces = pieces
        self.raw = core.sb(f"{tag}_raw", [P, raw_slots, kts, P], F32, ctx)
        self.hi = core.sb(f"{tag}_hi", [P, slots, kts, P], F32R, ctx)
        self.lo = core.sb(f"{tag}_lo", [P, slots, kts, P], F32R, ctx)
        self.hi_made, self.split, self.open = core.sems(f"{tag}_hi_made {tag}_split {tag}_open")
        self.loaded = core.sems(" ".join(f"{tag}_loaded{i}" for i in range(raw_slots)))

    def load(self, sp, u, t, src):
        n = self.per_unit * u + t
        at_least(sp, self.split, n - self.raw_slots + 1)
        sp.dma_start(self.raw[:, t % self.raw_slots], src).then_inc(self.loaded[t % self.raw_slots], 16)

    def make(self, pool, u, t, read, reads, piece=None):
        n, s, r = self.per_unit * u + t, t % self.slots, t % self.raw_slots
        loads = (self.per_unit // self.raw_slots) * u + t // self.raw_slots + 1
        width = self.kts // self.pieces
        for j in range(self.pieces) if piece is None else (piece,):
            part = slice(width * j, width * (j + 1))
            if j == 0:
                pool.wait_ge(self.loaded[r], 16 * loads)
                at_least(pool, read, reads)
                plain_wait(pool, self.open)
            pool.tensor_scalar(self.hi[:, s, part], self.raw[:, r, part], 1.0, 0.0, ALU.mult,
                               ALU.add).then_inc(self.hi_made, 1)
            pool.wait_ge(self.hi_made, self.pieces * n + j + 1)
            lo = pool.tensor_tensor(self.lo[:, s, part], self.raw[:, r, part], f32(self.hi[:, s, part]), ALU.subtract)
            if j == self.pieces - 1:
                lo.then_inc(self.split, 1)


class Projection:

    def __init__(self, core, ctx, tag, weights, ps, rhs, banks=NH):
        self.w, self.ps, self.rhs, self.banks = weights, ps, rhs, banks
        self.done, = core.sems(f"{tag}_done")
        self.free = core.sems(f"{tag}_free0 {tag}_free1")[:banks]

    def bank(self, h):
        h %= self.banks
        return self.ps[:, h * HALF:(h + 1) * HALF]

    def part(self, pe, u, t, h, kt, free=None):
        rhs_hi, rhs_lo = self.rhs
        n, s = self.w.per_unit * u + t, t % self.w.slots
        if kt == 0:
            if h == 0:
                pe.wait_ge(self.w.split, n + 1)
            if free is None:
                free = (self.free[h], n) if self.banks == NH else (self.free[0], NH * n + h)
            at_least(pe, *free)
        cols = slice(h * HALF, (h + 1) * HALF)
        mm = product(pe, self.bank(h), self.w.hi[:, s, kt], self.w.lo[:, s, kt], rhs_hi[:, kt, cols], rhs_lo[:, kt, cols],
                     start=(kt == 0), stop=(kt == self.w.kts - 1))
        if kt == self.w.kts - 1:
            mm.then_inc(self.done, 1)

    def run(self, pe, u, t, free=(None, None)):
        for h in range(NH):
            for kt in range(self.w.kts):
                self.part(pe, u, t, h, kt, free[h])

    def run_as_ready(self, pe, u, t, features):
        for kt in range(self.w.kts):
            features.wait(pe, kt)
            for h in range(NH):
                self.part(pe, u, t, h, kt)

    def weights(self, pool, u, t, piece=None):
        n = self.w.per_unit * u + t
        self.w.make(pool, u, t, self.done, NH * (n - self.w.slots + 1), piece)

    def freed(self, eng, u, t, h):
        n = self.w.per_unit * u + t
        eng.wait_ge(*((self.free[h], n + 1) if self.banks == NH else (self.free[0], NH * n + h + 1)))



def merge_phase(core, b, w_in_t, w_branch_t, oT, gates, merged):
    tag = f"m{b}"
    early = EARLY_GATES[b]
    with core.phase() as ctx:
        o_hi = core.sb(f"{tag}_o_hi", [P, BT, S], F32R, ctx)
        o_lo = core.sb(f"{tag}_o_lo", [P, BT, S], F32R, ctx)
        sig = core.sb(f"{tag}_sig", [P, S], F32, ctx)
        last = core.sb(f"{tag}_last", [P, 2, S], F32, ctx)
        keep = b == 2
        total = core.R if keep else core.sb(f"{tag}_total", [P, 2, S], F32, ctx)
        early_gates = core.sb(f"{tag}_gates", [P, early, S], F32, ctx)
        WG = WeightStream(core, ctx, f"{tag}wg", 2, 2, 2)
        WY = WeightStream(core, ctx, f"{tag}wy", 2, 2, 2, kts=BT)
        gate = Projection(core, ctx, f"{tag}g", WG, core.ps[0], (core.hT_hi, core.hT_lo))
        y = Projection(core, ctx, f"{tag}y", WY, core.ps[1], (o_hi, o_lo))
        o_hi_ok, o_lo_ok, sig_ok, part_ok, sum_ok = core.sems(
            " ".join(f"{tag}_{n}" for n in "o_hi_ok o_lo_ok sig_ok part_ok sum_ok".split()))
        last_in = core.sems(f"{tag}_last_in0 {tag}_last_in1")
        stored = core.sems(f"{tag}_stored0 {tag}_stored1")
        gates_in, = core.sems(f"{tag}_gates_in")

        def gate_index(u, t):
            slot = (t - early) % 2
            return u + (t - early - slot) // 2, slot

        def is_early(u, t):
            return 2 * u + t < early

        block = ctx.enter_context(core.nc.Block())

        @block.sync
        def _(sp):
            def unit(u):
                for t in range(2):
                    if not is_early(u, t):
                        WG.load(sp, *gate_index(u, t), w_in_t[GATE_TILE[b] + 2 * u + t])
                    WY.load(sp, u, t, w_branch_t[b, 2 * u + t])
                    if b:
                        at_least(sp, sum_ok, NH * (2 * u + t - 1))
                        sp.dma_start(last[:, t], merged[b - 1, 2 * u + t]).then_inc(last_in[t], 16)

            def store(u):
                for t in range(2):
                    sp.wait_ge(sum_ok, NH * (2 * u + t + 1))
                    sp.dma_start(merged[b, 2 * u + t], total[:, t]).then_inc(stored[t], 16)

            if keep:
                store = lambda u: None
            unit(0)
            sp.dma_start(early_gates[:], gates.rearrange("n p s -> p n s")).then_inc(gates_in, 16)
            unit(1)
            store(0)
            for u in range(2, KT // 2):
                unit(u)
                store(u - 1)
            store(KT // 2 - 1)
            for t in range(0 if keep else 2):
                sp.wait_ge(stored[t], 16 * (KT // 2))

        @block.gpsimd
        def _(pool):
            def unit(u):
                for t in range(2):
                    if not is_early(u, t):
                        gate.weights(pool, *gate_index(u, t))
                    y.weights(pool, u, t)

            for u in range(KT // 2):
                unit(u)

        @block.scalar
        def _(act):
            for k in range(BT):
                act.activation(o_hi[:, k], oT[:, k], ACT.Copy).then_inc(o_hi_ok, 1)

            def unit(u):
                for t in range(2):
                    for h in range(NH):
                        g = NH * (2 * u + t) + h
                        cols = slice(h * HALF, (h + 1) * HALF)
                        if not is_early(u, t):
                            act.wait_ge(gate.done, g - NH * early + 1)
                        at_least(act, part_ok, g - 1)
                        logits = early_gates[:, 2 * u + t, cols] if is_early(u, t) else gate.bank(h)
                        act.activation(sig[:, cols], logits, ACT.Sigmoid).then_inc(sig_ok, 1)

            act.wait_ge(gates_in, 16)
            for u in range(KT // 2):
                unit(u)

        @block.vector
        def _(dve):
            for k in range(BT):
                dve.wait_ge(o_hi_ok, k + 1)
                dve.tensor_tensor(o_lo[:, k], oT[:, k], f32(o_hi[:, k]), ALU.subtract).then_inc(o_lo_ok, 1)

            def unit(u):
                for t in range(2):
                    for h in range(NH):
                        g = NH * (2 * u + t) + h
                        cols = slice(h * HALF, (h + 1) * HALF)
                        dve.wait_ge(sig_ok, g + 1)
                        dve.wait_ge(y.done, g + 1)
                        slot = 2 * u + t if keep else t
                        if not keep:
                            at_least(dve, stored[t], 16 * u)
                        part = dve.tensor_tensor(total[:, slot, cols], y.bank(h), sig[:, cols], ALU.mult)
                        part.then_inc(part_ok, 1)
                        dve.wait_ge(part_ok, g + 1)
                        if b:
                            dve.wait_ge(last_in[t], 16 * (u + 1))
                            dve.tensor_tensor(total[:, slot, cols], total[:, slot, cols], last[:, t, cols],
                                              ALU.add).then_inc(sum_ok, 1)
                        else:
                            dve.sem_inc(sum_ok, 1)

            for u in range(KT // 2):
                unit(u)

        @block.tensor
        def _(pe):
            def unit(u):
                for t in range(2):
                    n = 2 * u + t
                    if not is_early(u, t):
                        gate.run(pe, *gate_index(u, t), [(sig_ok, NH * (n - 1) + h + 1) for h in range(NH)])
                    if n == 0:
                        for kt in range(BT):
                            pe.wait_ge(o_lo_ok, kt + 1)
                            for h in range(NH):
                                y.part(pe, 0, 0, h, kt, (part_ok, 0))
                        continue
                    y.run(pe, u, t, [(part_ok, NH * (n - 1) + h + 1) for h in range(NH)])

            for u in range(KT // 2):
                unit(u)


def out_phase(core, w_out_t, xT):
    nc = core.nc
    with core.phase() as ctx:
        W = WeightStream(core, ctx, "ow", 2, 2, 2)
        proj = Projection(core, ctx, "op", W, core.ps[0], (core.hT_hi, core.hT_lo))
        x_in = core.sems("out_x_in0 out_x_in1")
        x = core.sb("out_x", [P, 2, S], F32, ctx)
        sq = core.sb("out_sq", [P, 2, S], F32, ctx)
        acc = core.sb("out_acc", [P, S], F32, ctx)
        merged = Features(core, "out", lambda kt: core.R[:, kt])
        rms = Rms(core, "out", lambda kt: core.R[:, kt], (sq[:, 0], sq[:, 1]), acc[:], core.ps[1], core.rstd[:])
        block = ctx.enter_context(nc.Block())

        @block.sync
        def _(sp):
            def load(kt):
                W.load(sp, kt // 2, kt % 2, w_out_t[kt])
                if kt >= 2:
                    sp.wait_ge(proj.free[1], kt - 1)
                sp.dma_start(x[:, kt % 2], xT[:, kt]).then_inc(x_in[kt % 2], 16)

            for kt in range(KT):
                load(kt)

        @block.gpsimd
        def _(pool):
            for t in range(2):
                proj.weights(pool, 0, t)
            merged.on_pool(pool)
            with pool.Fori(1, KT // 2) as u:
                for t in range(2):
                    proj.weights(pool, u, t)

        @block.scalar
        def _(act):
            act.preload_act_table_set(EXP_LN)
            for kt in range(KT):
                merged.hi(act, kt)
            for kt in range(KT):
                for h in range(NH):
                    proj.freed(act, kt // 2, kt % 2, h)
                rms.square(act, kt)
            rms.root(act)

        @block.vector
        def _(dve):
            for kt in range(KT):
                merged.on_dve(dve, kt)
            merged.wait(dve, KT - 1)
            for kt in range(KT):
                dve.wait_ge(x_in[kt % 2], 16 * (kt // 2 + 1))
                for h in range(NH):
                    cols = slice(h * HALF, (h + 1) * HALF)
                    dve.wait_ge(proj.done, NH * kt + h + 1)
                    dve.tensor_tensor(core.R[:, kt, cols], proj.bank(h), x[:, kt % 2, cols],
                                      ALU.add).then_inc(proj.free[h], 1)
                rms.add(dve, kt)

        @block.tensor
        def _(pe):
            proj.run_as_ready(pe, 0, 0, merged)
            proj.run(pe, 0, 1)
            with pe.Fori(1, KT // 2) as u:
                for t in range(2):
                    proj.run(pe, u, t)
            rms.sum(pe)



def mlp_phase(core, w_up_t, w_down_t, conv_in, work, out):
    nc = core.nc
    GROUPS = KT * NH
    UNITS_F = FT // 2
    with core.phase() as ctx:
        WU = WeightStream(core, ctx, "fu", 4, 2, 2)
        WD = WeightStream(core, ctx, "fd", 2, 2, 2)
        up = [Projection(core, ctx, f"f{n}", WU, core.ps[i], (core.hT_hi, core.hT_lo))
              for i, n in enumerate("gv")]
        y2 = core.sb("f_y2", [P, 3, S], F32, ctx)
        norm = Normalize(core, "n2", 1, lambda kt: core.R[:, kt], core.rstd[:], [y2[:, i] for i in range(3)])
        raw = [W.raw[:, i].rearrange("p k f -> p (k f)") for W in (WU, WD) for i in range(2)]
        result = [work[:, i] for i in range(4)] + [y2[:, i] for i in range(3)] + [raw[3]]
        rms = Rms(core, "n3", lambda kt: core.R[:, kt], (raw[0], raw[1]), raw[2], core.ps[0], core.rstd[:])
        y3_ready, stored = core.sems("f_y3_ready f_stored")
        conv_w = core.sb("f_conv_w", [P, 2 * FT, 4], F32, ctx)
        taps = core.sb("f_taps", [P, 2, 4], F32, ctx)
        c = work[:].rearrange("p (slot i) s -> p slot i s", i=2)
        a_hi = core.sb("f_a_hi", [P, 2, S], F32R, ctx)
        a_lo = core.sb("f_a_lo", [P, 2, S], F32R, ctx)
        (conv_loaded, taps_ok, c0_ok, c1_ok, c2_ok, silu_ok, a_ok, a_hi_ok, a_lo_ok, down_ps, down_sum) = core.sems(" ".join("f_" + n for n in (
             "conv_loaded taps_ok c0_ok c1_ok c2_ok silu_ok a_ok a_hi_ok a_lo_ok down_ps down_sum").split()))
        block = ctx.enter_context(nc.Block())

        def down_bank(g):
            return core.ps[2 + g % 4 // 2][:, (g % 2) * HALF:(g % 2 + 1) * HALF]

        @block.sync
        def _(sp):
            def unit(u):
                for t in range(2):
                    WU.load(sp, u, 2 * t, w_up_t[2 * u + t])
                    WU.load(sp, u, 2 * t + 1, w_up_t[2 * u + t + FT])
                    if is_first(u) and t == 0:
                        sp.dma_start(conv_w[:], conv_in).then_inc(conv_loaded, 16)
                for t in range(2):
                    WD.load(sp, u, t, w_down_t[2 * u + t])

            unit(0)
            with sp.Fori(1, UNITS_F) as u:
                unit(u)
            for kt in range(KT):
                sp.wait_ge(y3_ready, kt + 1)
                sp.dma_start(out[:, kt], result[kt]).then_inc(stored, 16)
            sp.wait_ge(stored, 16 * KT)

        @block.gpsimd
        def _(pool):
            def unit(u):
                for t in range(2):
                    for i in range(2):
                        WU.make(pool, u, 2 * t + i, up[i].done, NH * (2 * u + t))
                    if is_first(u) and t == 0:
                        norm.features.on_pool(pool)
                for t in range(2):
                    WD.make(pool, u, t, down_ps, GROUPS * u)

            unit(0)
            with pool.Fori(1, UNITS_F) as u:
                unit(u)

        @block.scalar
        def _(act):
            norm.on_act(act)

            def unit(u):
                for t in range(2):
                    f = 2 * u + t
                    for i in range(2):
                        n = 2 * f + i
                        act.wait_ge(up[i].done, NH * (f + 1))
                        act.wait_ge(taps_ok, n + 1)
                        at_least(act, a_lo_ok, f - 1)
                        act.activation(c[:, t, i], core.ps[i][:], ACT.Identity, bias=taps[:, i, 3:4],
                                       scale=taps[:, i, 2:3]).then_inc(c0_ok, 1)
                        if i == 0:
                            act.wait_ge(c2_ok, n + 1)
                            act.activation(c[:, t, 0], c[:, t, 0], ACT.Silu).then_inc(silu_ok, 1)
                    act.wait_ge(a_ok, f + 1)
                    at_least(act, down_ps, GROUPS * u)
                    act.activation(a_hi[:, t], c[:, t, 0], ACT.Copy).then_inc(a_hi_ok, 1)

            unit(0)
            with act.Fori(1, UNITS_F) as u:
                unit(u)
            act.preload_act_table_set(EXP_LN)
            for kt in range(KT):
                act.wait_ge(down_sum, GROUPS * (UNITS_F - 1) + NH * (kt + 1))
                rms.square(act, kt)
            rms.root(act)

        def sum_down(dve, u, last=False):
            for g in range(GROUPS):
                d, h = g // NH, g % NH
                cols = slice(h * HALF, (h + 1) * HALF)
                dve.wait_ge(down_ps, GROUPS * u + g + 1)
                dve.tensor_tensor(core.R[:, d, cols], down_bank(g), core.R[:, d, cols], ALU.add).then_inc(down_sum, 1)
                if last and h == 1 and d:
                    rms.add(dve, d - 1)

        @block.vector
        def _(dve):
            norm.on_dve(dve)
            dve.wait_ge(conv_loaded, 16)

            def unit(u):
                for t in range(2):
                    f = 2 * u + t
                    for i in range(2):
                        n = 2 * f + i
                        at_least(dve, c2_ok, n - 1)
                        dve.tensor_copy(taps[:, i], conv_w[:, f + FT * i]).then_inc(taps_ok, 1)
                    for i in range(2):
                        n = 2 * f + i
                        dve.wait_ge(c0_ok, n + 1)
                        for lag, done in ((1, c1_ok), (2, c2_ok)):
                            if lag == 2:
                                dve.wait_ge(c1_ok, n + 1)
                            dve.scalar_tensor_tensor(out=c[:, t, i, lag:S], in0=core.ps[i][:, 0:S - lag],
                                                     scalar=taps[:, i, 2 - lag:3 - lag], in1=c[:, t, i, lag:S],
                                                     op0=ALU.mult, op1=ALU.add).then_inc(done, 1)
                    if t == 0 and not is_first(u):
                        sum_down(dve, u - 1)
                    dve.wait_ge(silu_ok, f + 1)
                    dve.wait_ge(c2_ok, 2 * f + 2)
                    dve.tensor_tensor(c[:, t, 0], c[:, t, 0], c[:, t, 1], ALU.mult).then_inc(a_ok, 1)
                    dve.wait_ge(a_hi_ok, f + 1)
                    dve.tensor_tensor(a_lo[:, t], c[:, t, 0], f32(a_hi[:, t]), ALU.subtract).then_inc(a_lo_ok, 1)

            unit(0)
            with dve.Fori(1, UNITS_F) as u:
                unit(u)
            sum_down(dve, UNITS_F - 1, last=True)
            rms.add(dve, KT - 1)
            dve.wait_ge(rms.ready, 1)
            for kt in range(KT):
                dve.scalar_tensor_tensor(out=result[kt], in0=core.R[:, kt], scalar=core.normw[:, 2, kt:kt + 1],
                                         in1=core.rstd[:], op0=ALU.mult, op1=ALU.mult).then_inc(y3_ready, 1)

        @block.tensor
        def _(pe):
            def down(u):
                pe.wait_ge(a_lo_ok, 2 * (u + 1))
                pe.wait_ge(WD.split, 2 * (u + 1))
                for g in range(GROUPS):
                    d, h = g // NH, g % NH
                    cols = slice(h * HALF, (h + 1) * HALF)
                    at_least(pe, down_sum, GROUPS * u + g - 3)
                    for t in range(2):
                        mm = product(pe, down_bank(g), WD.hi[:, t, d], WD.lo[:, t, d], a_hi[:, t, cols],
                                     a_lo[:, t, cols], t == 0, t == 1)
                    mm.then_inc(down_ps, 1)

            def unit(u):
                for t in range(2):
                    f = 2 * u + t
                    if is_first(u) and t == 0:
                        for kt in range(KT):
                            norm.features.wait(pe, kt)
                            for i in range(2):
                                for h in range(NH):
                                    up[i].part(pe, 0, i, h, kt, (c2_ok, 0))
                        continue
                    for i in range(2):
                        up[i].run(pe, u, 2 * t + i, [(c2_ok, 2 * (f - 1) + i + 1)] * NH)
                    if t == 0 and not is_first(u):
                        down(u - 1)

            unit(0)
            unit(1)
            with pe.Fori(2, UNITS_F) as u:
                unit(u)
            down(UNITS_F - 1)
            rms.sum(pe)



SB_STEPS = [(c, j, h) for c in range(NH) for j in range(4 * c + 3, -1, -1) for h in range(2)]


def sb_columns(c, j):
    t0 = max(HALF * c, P * j)
    return t0, HALF * (c + 1) - t0


def stick_breaking_phase(core, dram, oT, gates):
    nc, w_in = core.nc, dram["w_in_t"]
    NZ, NE, NS, NW = 4, 3, 4, 3
    TRI, REST, PV = 2, 4, 6
    ARG, W_LO = 2, 4
    W_EXP = 3
    W_HI = 3
    HALF_STEPS = SB_STEPS.index((1, 7, 0))
    with core.phase() as ctx:
        W = WeightStream(core, ctx, "sbw", 3, 3, 1, pieces=4)
        proj = Projection(core, ctx, "sbp", W, core.ps[3], (core.hT_hi, core.hT_lo))
        gates_out, = core.sems("sb_gates_out")
        (masks_in, qk_hi_ok, qk_lo_ok, v_turned, v_hi_ok, v_lo_ok, pads_ok,
         z_ok, zc_ok, cap_ok, e_ok, l_ok, sp_ok, sp_hi_ok, sp_lo_ok, tri_ok, arg_ok, rest_ok,
         w_ok, w_hi_ok, w_lo_ok, pv_ok, o_read) = core.sems(" ".join("sb_" + n for n in (
                "masks_in qk_hi_ok qk_lo_ok v_turned v_hi_ok v_lo_ok pads_ok z_ok zc_ok cap_ok e_ok l_ok "
                "sp_ok sp_hi_ok sp_lo_ok tri_ok arg_ok rest_ok w_ok w_hi_ok w_lo_ok pv_ok o_read").split()))
        qk_hi = core.sb("sb_qk_hi", [P, 2, S], F32R, ctx)
        qk_lo = core.sb("sb_qk_lo", [P, 2, S], F32R, ctx)
        v_hi = core.sb("sb_v_hi", [P, NT, 3, DH], F32R, ctx)
        v_lo = core.sb("sb_v_lo", [P, NT, 3, DH], F32R, ctx)
        zc = core.sb("sb_zc", [P, NZ, HALF], F32, ctx)
        e = core.sb("sb_e", [P, NE, HALF], F32, ctx)
        sp_hi = core.sb("sb_sp_hi", [P, NS, HALF], F32R, ctx)
        sp_lo = core.sb("sb_sp_lo", [P, NS, HALF], F32R, ctx)
        w = core.sb("sb_w", [P, NW, HALF], F32, ctx)
        w_hi = core.sb("sb_w_hi", [P, NW, HALF], F32R, ctx)
        w_lo = core.sb("sb_w_lo", [P, NW, HALF], F32R, ctx)
        mask_raw = core.sb("sb_mask_raw", [P, 4, P], F32, ctx)
        mask = core.sb("sb_mask", [P, 4, P], F32R, ctx)
        stage = core.sb("sb_stage", [P, 3, S], F32, ctx)
        z_ps, c_ps, o_ps = core.ps[0], core.ps[1], core.ps[2]
        K = len(SB_STEPS)
        block = ctx.enter_context(nc.Block())

        @block.sync
        def _(sp):
            sp.dma_start(mask_raw[:], dram["sb_masks"]).then_inc(masks_in, 16)

            def load(u, t):
                W.load(sp, u, t, w_in[GATE_TILE[1] + t if is_gates(u) else SB_TILES[t] + u])

            for t in range(3):
                load(0, t)
            load(1, 0)

            def unit(u):
                load(u + 1, 1)
                load(u + 1, 2)
                load(u + 2, 0)

            unit(0)
            with sp.Fori(1, UNITS - 2) as u:
                unit(u)
            unit(UNITS - 2)
            load(UNITS, 1)
            load(UNITS, 2)
            store_gates(sp, proj, stage, gates, gates_out)

        @block.gpsimd
        def _(pool):
            pool.memset(f32(v_hi[:, :, 1]), 0.0)
            pool.memset(f32(v_lo[:, :, 1]), 0.0).then_inc(pads_ok, 1)
            pool.wait_ge(masks_in, 16)
            pool.tensor_scalar(mask[:], mask_raw[:], 1.0, 0.0, ALU.mult, ALU.add).then_inc(pads_ok, 1)

            for t in range(3):
                proj.weights(pool, 0, t)
            proj.weights(pool, 1, 0)

            def unit(u, last=False):
                for k in range(K + W_HI):
                    if k % 2 == 0 and k < (16 if last else K):
                        v, t = ((u + 1, 1), (u + 1, 2), (u + 2, 0))[k // 8]
                        proj.weights(pool, v, t, piece=k % 8 // 2)
                    if k >= W_HI:
                        m = k - W_HI
                        n = sb_columns(*SB_STEPS[m][:2])[1]
                        pool.wait_ge(w_ok, K * u + m + 1)
                        at_least(pool, pv_ok, K * u + m - NW + 1)
                        plain_wait(pool, W.open)
                        pool.tensor_scalar(w_hi[:, m % NW, 0:n], w[:, m % NW, 0:n], 1.0, 0.0,
                                           ALU.mult, ALU.add).then_inc(w_hi_ok, 1)
                    if k < K:
                        n = sb_columns(*SB_STEPS[k][:2])[1]
                        pool.wait_ge(sp_ok, K * u + k + 1)
                        at_least(pool, rest_ok, K * u + k - NS + 1)
                        plain_wait(pool, W.open)
                        pool.tensor_scalar(sp_hi[:, k % NS, 0:n], e[:, k % NE, 0:n], 1.0, 0.0,
                                           ALU.mult, ALU.add).then_inc(sp_hi_ok, 1)
                        pool.wait_ge(sp_hi_ok, K * u + k + 1)
                        pool.tensor_tensor(sp_lo[:, k % NS, 0:n], e[:, k % NE, 0:n],
                                           f32(sp_hi[:, k % NS, 0:n]), ALU.subtract).then_inc(sp_lo_ok, 1)

            unit(0)
            with pool.Fori(1, UNITS - 1) as u:
                unit(u)
            unit(UNITS - 1, last=True)

        @block.scalar
        def _(act):
            act.preload_act_table_set(EXP_LN)
            def next_half(u, g):
                t, h = g // NH, g % NH
                act.wait_ge(qk_lo_ok, 2 * u)
                act.wait_ge(v_turned, NH * u)
                stage_half(act, proj, stage[:, t], u, t, h, QK_SCALE if t == 0 and not is_gates(u) else 1.0)

            for g in range(3 * NH):
                stage_half(act, proj, stage[:, g // NH], 0, g // NH, g % NH, QK_SCALE if g < NH else 1.0)

            def split_qk(u):
                for t in range(2):
                    for h in range(NH):
                        proj.freed(act, u, t, h)
                    at_least(act, z_ok, K * u)
                    act.activation(qk_hi[:, t], stage[:, t], ACT.Copy).then_inc(qk_hi_ok, 1)

            split_qk(0)

            def unit(u, last=False):
                for h in range(NH):
                    act.wait_ge(v_turned, NH * u + h + 1)
                    at_least(act, pv_ok, K * u)
                    act.activation(v_hi[:, 4 * h:4 * h + 4, 0:3:2, :],
                                   z_ps[:, h * HALF:(h + 1) * HALF].rearrange("p (a b c) -> p a b c", a=4, b=2),
                                   ACT.Copy).then_inc(v_hi_ok, 1)
                act.wait_ge(v_lo_ok, NH * (u + 1))
                for k in range(K + W_EXP):
                    if k < K:
                        n = sb_columns(*SB_STEPS[k][:2])[1]
                        act.wait_ge(z_ok, K * u + k + 1)
                        at_least(act, arg_ok, K * u + k - NZ + 1)
                        act.activation(zc[:, k % NZ, 0:n], z_ps[:, (k % 2) * HALF:(k % 2) * HALF + n],
                                       ACT.Copy).then_inc(zc_ok, 1)
                    if k >= W_EXP:
                        m = k - W_EXP
                        n = sb_columns(*SB_STEPS[m][:2])[1]
                        act.wait_ge(arg_ok, K * u + m + 1)
                        act.activation(w[:, m % NW, 0:n], w[:, m % NW, 0:n], ACT.Exp).then_inc(w_ok, 1)
                    if k < K:
                        n = sb_columns(*SB_STEPS[k][:2])[1]
                        act.wait_ge(cap_ok, K * u + k + 1)
                        act.activation(e[:, k % NE, 0:n], e[:, k % NE, 0:n], ACT.Exp).then_inc(e_ok, 1)
                        act.wait_ge(e_ok, K * u + k + 1)
                        act.activation(e[:, k % NE, 0:n], e[:, k % NE, 0:n], ACT.Ln,
                                       bias=1.0).then_inc(l_ok, 1)
                    if k % 4 == 1 and k >= 5:
                        next_half(u + 1, (k - 5) // 4)
                    if k == HALF_STEPS + PV + 1:
                        act.wait_ge(pv_ok, K * u + HALF_STEPS)
                        act.activation(oT[:, u, 0:HALF], o_ps[:, 0:HALF], ACT.Copy).then_inc(o_read, 1)
                if not last:
                    split_qk(u + 1)
                act.wait_ge(pv_ok, K * (u + 1))
                act.activation(oT[:, u, HALF:S], o_ps[:, HALF:S], ACT.Copy).then_inc(o_read, 1)

            unit(0)
            with act.Fori(1, UNITS - 1) as u:
                unit(u)
            unit(UNITS - 1, last=True)

        @block.vector
        def _(dve):
            def split_qk(u):
                for t in range(2):
                    dve.wait_ge(qk_hi_ok, 2 * u + t + 1)
                    dve.tensor_tensor(qk_lo[:, t], stage[:, t], f32(qk_hi[:, t]), ALU.subtract).then_inc(qk_lo_ok, 1)

            split_qk(0)

            def unit(u, last=False):
                for h in range(NH):
                    dve.wait_ge(v_hi_ok, NH * u + h + 1)
                    dve.tensor_tensor(v_lo[:, 4 * h:4 * h + 4, 0:3:2, :],
                                      z_ps[:, h * HALF:(h + 1) * HALF].rearrange("p (a b c) -> p a b c", a=4, b=2),
                                      f32(v_hi[:, 4 * h:4 * h + 4, 0:3:2, :]), ALU.subtract).then_inc(v_lo_ok, 1)
                for k in range(K + W_LO):
                    if k < K:
                        n = sb_columns(*SB_STEPS[k][:2])[1]
                        dve.wait_ge(zc_ok, K * u + k + 1)
                        at_least(dve, sp_lo_ok, K * u + k - NE + 1)
                        dve.tensor_scalar(e[:, k % NE, 0:n], zc[:, k % NZ, 0:n], EXP_CAP, None,
                                          ALU.min).then_inc(cap_ok, 1)
                    if ARG <= k < K + ARG:
                        m = k - ARG
                        c, j, h = SB_STEPS[m]
                        t0, n = sb_columns(c, j)
                        dve.wait_ge(tri_ok, K * u + m + 1)
                        at_least(dve, w_lo_ok, K * u + m - NW + 1)
                        dve.tensor_tensor(w[:, m % NW, 0:n], zc[:, m % NZ, 0:n],
                                          c_ps[:, h * HALF + HALF - n:(h + 1) * HALF],
                                          ALU.subtract).then_inc(arg_ok, 1)
                    if k >= W_LO:
                        m = k - W_LO
                        n = sb_columns(*SB_STEPS[m][:2])[1]
                        dve.wait_ge(w_hi_ok, K * u + m + 1)
                        at_least(dve, pv_ok, K * u + m - NW + 1)
                        dve.tensor_tensor(w_lo[:, m % NW, 0:n], w[:, m % NW, 0:n],
                                          f32(w_hi[:, m % NW, 0:n]), ALU.subtract).then_inc(w_lo_ok, 1)
                    if k < K:
                        n = sb_columns(*SB_STEPS[k][:2])[1]
                        dve.wait_ge(l_ok, K * u + k + 1)
                        dve.tensor_tensor(e[:, k % NE, 0:n], e[:, k % NE, 0:n], zc[:, k % NZ, 0:n],
                                          ALU.max).then_inc(sp_ok, 1)
                if not last:
                    split_qk(u + 1)

            unit(0)
            with dve.Fori(1, UNITS - 1) as u:
                unit(u)
            unit(UNITS - 1, last=True)

        @block.tensor
        def _(pe):
            for t in range(3):
                proj.run(pe, 0, t)

            def turn(u):
                for h in range(NH):
                    proj.freed(pe, u, 2, h)
                at_least(pe, zc_ok, K * u)
                turn_v(pe, stage[:, 2], z_ps, core.ident[:], v_turned)

            turn(0)

            def unit(u, last=False):
                if isinstance(u, int):
                    pe.wait_ge(pads_ok, 2)
                pe.wait_ge(v_lo_ok, NH * (u + 1))
                pe.wait_ge(qk_lo_ok, 2 * (u + 1))
                for k in range(K + PV):
                    if k < K:
                        c, j, h = SB_STEPS[k]
                        t0, n = sb_columns(c, j)
                        rows, bank = slice(DH * h, DH * (h + 1)), (k % 2) * HALF
                        at_least(pe, zc_ok, K * u + k - 1)
                        mm = product(pe, z_ps[:, bank:bank + n],
                                     qk_hi[rows, 1, P * j:P * (j + 1)], qk_lo[rows, 1, P * j:P * (j + 1)],
                                     qk_hi[rows, 0, t0:t0 + n], qk_lo[rows, 0, t0:t0 + n], True, j < 4 * c)
                        if j >= 4 * c:
                            mm = pe.matmul(z_ps[:, bank:bank + P], mask[:, 0], mask[:, 3],
                                           start=False, stop=True, skip_group_check=True)
                        mm.then_inc(z_ok, 1)
                    if k < K:
                        for part in (2 * k, 2 * k + 1):
                            g, kt = part // KT, part % KT
                            proj.part(pe, u + 1, g // NH, g % NH, kt)
                    if REST <= k < K + REST:
                        m = k - REST
                        c, j, h = SB_STEPS[m]
                        n = sb_columns(c, j)[1]
                        pe.wait_ge(arg_ok, K * u + m + 1)
                        for part in (sp_hi, sp_lo):
                            mm = pe.matmul(c_ps[:, (h + 1) * HALF - n:(h + 1) * HALF], mask[:, 2],
                                           part[:, m % NS, 0:n], start=False, stop=(j == 0),
                                           skip_group_check=True)
                        mm.then_inc(rest_ok, 1)
                    if TRI <= k < K + TRI:
                        m = k - TRI
                        c, j, h = SB_STEPS[m]
                        n = sb_columns(c, j)[1]
                        pe.wait_ge(sp_lo_ok, K * u + m + 1)
                        for part in (sp_hi, sp_lo):
                            mm = pe.matmul(c_ps[:, (h + 1) * HALF - n:(h + 1) * HALF], mask[:, 1],
                                           part[:, m % NS, 0:n],
                                           start=(j == 4 * c + 3 and part is sp_hi), stop=False,
                                           skip_group_check=True)
                        mm.then_inc(tri_ok, 1)
                    if k >= PV:
                        m = k - PV
                        c, j, h = SB_STEPS[m]
                        t0, n = sb_columns(c, j)
                        if m in (0, HALF_STEPS):
                            at_least(pe, o_read, NH * u + c - 1)
                        pe.wait_ge(w_lo_ok, K * u + m + 1)
                        mm = product(pe, o_ps[:, t0:t0 + n], v_hi[:, j, h:h + 2], v_lo[:, j, h:h + 2],
                                     w_hi[:, m % NW, 0:n], w_lo[:, m % NW, 0:n],
                                     (j == 4 * c + 3 and h == 0), (j == 0 and h == 1))
                        mm.then_inc(pv_ok, 1)
                    if k == K + PV - 2 and not last:
                        turn(u + 1)

            unit(0)
            with pe.Fori(1, UNITS - 1) as u:
                unit(u)
            unit(UNITS - 1, last=True)



def turn_v(pe, vT, ps, ident, turned):
    for h in range(NH):
        for a in range(4):
            col = h * HALF + a * P
            mm = pe.transpose(ps[:, col:col + P], vT[:, col:col + P], ident)
        mm.then_inc(turned, 1)


def store_gates(sp, proj, stage, gates, gates_out):
    tiles = proj.w.per_unit
    for t in range(tiles):
        for h in range(NH):
            proj.freed(sp, UNITS, t, h)
        sp.dma_start(gates[t], stage[:, t]).then_inc(gates_out, 16)
    sp.wait_ge(gates_out, 16 * tiles)


def stage_half(act, proj, stage, u, t, h, scale=1.0):
    act.wait_ge(proj.done, NH * (proj.w.per_unit * u + t) + h + 1)
    act.activation(stage[:, h * HALF:(h + 1) * HALF], proj.bank(h), ACT.Copy,
                   scale=scale).then_inc(proj.free[h % proj.banks], 1)



def hgrn2_phase(core, dram, oT, gates):
    nc, w_in = core.nc, dram["w_in_t"]
    F, V, Q, G = range(4)
    TILES = [HG_TILES[i] for i in (1, 2, 0, 3)]
    STEPS = LEVELS + 1
    with core.phase() as ctx:
        W = WeightStream(core, ctx, "hgw", 4, 2, 2, pieces=4)
        proj = Projection(core, ctx, "hgp", W, core.ps[3], (core.hT_hi, core.hT_lo))
        names = ("small_in nab_ok ez_ok lz_ok logf_ok cum_ok sp_ok key_ok q_ok v_turned v_hi_ok "
                 "v_lo_ok gn_ok ge_ok gl_ok ga_ok gs_ok silu_ok kd_d kd_e kd_ok kd_turned kdT_hi_ok kq_ok "
                 "kdT_lo_ok upd_ok el_ok state_ok state_hi_ok state_lo_ok lev_d lev_e lev_x lev_hi lev_lo step_ps "
                 "score_ok s_hi_ok s_lo_ok qe_e qe_ok qe_hi_ok qe_lo_ok out_ps sq_ok ss_ok ln_ok rstd_ok rg_ok o_ok "
                 "zeroed const_in").split()
        sem = dict(zip(names, core.sems(" ".join("hg_" + n for n in names))))
        gates_out, = core.sems("hg_gates_out")
        stage = core.sb("hg_stage", [P, 4, S], F32, ctx)
        work = core.sb("hg_work", [P, 8, S], F32, ctx)
        e, cum, key, q, gz = (work[:, i] for i in range(5))
        x = work[:, 5:8]
        xq, xo = x[:, 1], x[:, 2]
        score = core.sb("hg_score", [P, NT, P], F32, ctx)
        state = core.sb("hg_state", [P, NT, P], F32, ctx)
        elast = core.sb("hg_elast", [P, NT], F32, ctx)
        levels = core.sb("hg_levels", [P, LEVELS + 1, P], I32, ctx)
        onorm = core.sb("hg_onorm", [P, 1], F32, ctx)
        v_hi, v_lo = (core.sb(f"hg_v_{p}", [P, NT, P], F32R, ctx) for p in ("hi", "lo"))
        pair_hi, pair_lo = (core.sb(f"hg_pair_{p}", [P, 3, S], F32R, ctx) for p in ("hi", "lo"))
        SCORES, STATES, DECAYED, TURNED = 0, 1, 2, 2
        t_ps, k_ps, o_ps = core.ps[0], core.ps[1], core.ps[2]
        chunks = lambda ap: ap.rearrange("p (c t) -> p c t", t=P)
        flat = lambda t: t[:].rearrange("p c t -> p (c t)")
        x_tile = lambda kt: (stage[:, kt] if kt < 4 else work[:, kt])
        x_in = core.sems(" ".join(f"hg_x_in{kt}" for kt in range(KT)))
        rms = Rms(core, "n1", x_tile, (work[:, 0], work[:, 1]), work[:, 2], core.ps[0], work[:, 3])
        norm = Normalize(core, "n1", 0, x_tile, work[:, 3], [work[:, i] for i in range(3)])
        block = ctx.enter_context(nc.Block())

        def slot(l):
            return (2 - l) % 3

        def halves(ap, l):
            return ap.rearrange("p (b two t) -> p b two t", two=2, t=P >> (l + 1))

        @block.sync
        def _(sp):
            def load(u, t):
                W.load(sp, u, t, w_in[GATE_TILE[0] + t if is_gates(u) else TILES[t] + u])

            for kt in range(KT):
                sp.dma_start(x_tile(kt), dram["xT"][:, kt]).then_inc(x_in[kt], 16)
                if kt == 3:
                    load(0, F)
            for dst, src in ((core.ident, dram["ident"]), (core.normw, dram["norm_w"])):
                sp.dma_start(dst[:], src).then_inc(sem["const_in"], 16)
            sp.dma_start(levels[:], dram["hg_levels"]).then_inc(sem["small_in"], 16)
            sp.dma_start(onorm[:], dram["hg_onorm"]).then_inc(sem["small_in"], 16)
            for t in (V, Q, G):
                load(0, t)
            load(1, F)

            def unit(u):
                for t in (V, Q, G):
                    load(u + 1, t)
                load(u + 2, F)

            unit(0)
            with sp.Fori(1, UNITS - 2) as u:
                unit(u)
            unit(UNITS - 2)
            for t in (V, Q, G):
                load(UNITS, t)
            store_gates(sp, proj, stage, gates, gates_out)

        @block.gpsimd
        def _(pool):
            pool.memset(core.ones[:], 1.0)
            pool.memset(core.eps[:], EPS)
            pool.memset(score[:], 0.0)
            pool.memset(state[:, 0], 0.0).then_inc(sem["zeroed"], 1)

            def take_q(u):
                for h in range(NH):
                    proj.freed(pool, u, Q, h)
                at_least(pool, sem["qe_ok"], u)
                plain_wait(pool, W.open)
                pool.tensor_scalar(q, stage[:, Q], 1.0, 0.0, ALU.mult, ALU.add).then_inc(sem["q_ok"], 1)

            proj.weights(pool, 0, F)
            proj.weights(pool, 0, V)
            norm.features.on_pool(pool)
            proj.weights(pool, 0, Q)
            proj.weights(pool, 0, G)
            take_q(0)
            proj.weights(pool, 1, F)

            def unit(u, last=False):
                def split_weights(v, t, pieces):
                    for piece in pieces:
                        proj.weights(pool, v, t, piece=piece)

                split_weights(u + 1, V, range(4))
                split_weights(u + 1, Q, range(4))
                for l in range(LEVELS):
                    pool.wait_ge(sem["lev_hi"], LEVELS * u + l + 1)
                    pool.tensor_tensor(pair_lo[:, l % 3], x[:, slot(l)], f32(pair_hi[:, l % 3]),
                                       ALU.subtract).then_inc(sem["lev_lo"], 1)
                    if l in (2, 3):
                        split_weights(u + 1, G, (2 * l - 4, 2 * l - 3))
                    if l in (5, 6) and not last:
                        split_weights(u + 2, F, (2 * l - 10, 2 * l - 9))
                if not last:
                    take_q(u + 1)

            unit(0)
            with pool.Fori(1, UNITS - 1) as u:
                unit(u)
            unit(UNITS - 1, last=True)

        @block.scalar
        def _(act):
            act.preload_act_table_set(EXP_LN)
            for kt in range(KT):
                act.wait_ge(x_in[kt], 16)
                rms.square(act, kt)
            act.wait_ge(sem["zeroed"], 1)
            rms.root(act)
            norm.on_act(act)

            def stage_group(u, g):
                t = g // NH
                at_least(act, *((sem["sp_ok"], u), (sem["v_turned"], NH * u), (sem["q_ok"], u), (sem["silu_ok"], u))[t])
                stage_half(act, proj, stage[:, t], u, t, g % NH, HG_SCALE if t == Q and not is_gates(u) else 1.0)

            def softplus_tail(u):
                for h in range(NH):
                    proj.freed(act, u, F, h)
                at_least(act, sem["silu_ok"], u)
                act.activation(e, stage[:, F], ACT.Abs).then_inc(sem["nab_ok"], 1)
                act.wait_ge(sem["nab_ok"], u + 1)
                act.activation(e, e, ACT.Exp, scale=-1.0).then_inc(sem["ez_ok"], 1)
                act.wait_ge(sem["ez_ok"], u + 1)
                act.activation(e, e, ACT.Ln, bias=1.0).then_inc(sem["lz_ok"], 1)

            def make_key(u):
                act.wait_ge(sem["sp_ok"], u + 1)
                at_least(act, sem["lev_x"], LEVELS * u)
                act.activation(key, e, ACT.Exp, scale=-1.0).then_inc(sem["key_ok"], 1)

            def decay_keys(u):
                act.wait_ge(sem["cum_ok"], NT * (u + 1))
                at_least(act, sem["state_ok"], (NT - 1) * u)
                act.activation(elast[:], chunks(cum)[:, :, P - 1], ACT.Exp).then_inc(sem["el_ok"], 1)
                act.wait_ge(sem["kd_d"], u + 1)
                act.activation(x[:, 0], x[:, 0], ACT.Exp).then_inc(sem["kd_e"], 1)

            def split_v(u):
                for h in range(NH):
                    cols = slice(h * HALF, (h + 1) * HALF)
                    act.wait_ge(sem["v_turned"], NH * u + h + 1)
                    at_least(act, sem["out_ps"], NH * u)
                    act.activation(v_hi[:, 4 * h:4 * h + 4], chunks(t_ps[:, cols]), ACT.Copy).then_inc(sem["v_hi_ok"], 1)

            def decay(u, l):
                act.wait_ge(sem["lev_d"], LEVELS * u + l + 1)
                d = halves(x[:, slot(l)], l)
                act.activation(d[:, :, 0], d[:, :, 0], ACT.Exp, scale=-1.0)
                act.activation(d[:, :, 1], d[:, :, 1], ACT.Exp).then_inc(sem["lev_e"], 1)

            for g in range(2 * NH):
                stage_group(0, g)
            softplus_tail(0)
            for g in range(2 * NH, 4 * NH):
                stage_group(0, g)
            make_key(0)
            decay_keys(0)
            split_v(0)

            def unit(u, last=False):
                decay(u, 0)
                stage_group(u + 1, 0)
                act.wait_ge(sem["kd_turned"], u + 1)
                at_least(act, sem["out_ps"], NH * u)
                act.activation(pair_hi[:, TURNED], k_ps[:], ACT.Copy).then_inc(sem["kdT_hi_ok"], 1)
                for l in range(LEVELS):
                    if l + 1 < LEVELS:
                        decay(u, l + 1)
                    act.wait_ge(sem["lev_x"], LEVELS * u + l + 1)
                    if l == 2:
                        act.wait_ge(sem["upd_ok"], u + 1)
                    elif l >= 3:
                        act.wait_ge(sem["step_ps"], STEPS * u + l - 1)
                    act.activation(pair_hi[:, l % 3], x[:, slot(l)], ACT.Copy).then_inc(sem["lev_hi"], 1)
                    if l in (0, 1, 3, 4, 5):
                        stage_group(u + 1, {0: 1, 1: 2, 3: 3, 4: 4, 5: 5}[l])
                    if l == 2:
                        act.wait_ge(sem["step_ps"], STEPS * u + 1)
                        act.activation(e, stage[:, G], ACT.Abs).then_inc(sem["gn_ok"], 1)
                    if l == 3:
                        act.wait_ge(sem["gn_ok"], u + 1)
                        act.activation(e, e, ACT.Exp, scale=-1.0).then_inc(sem["ge_ok"], 1)
                    if l == 4:
                        act.wait_ge(sem["ge_ok"], u + 1)
                        act.activation(e, e, ACT.Ln, bias=1.0).then_inc(sem["gl_ok"], 1)
                    if l == 6:
                        act.wait_ge(sem["ga_ok"], u + 1)
                        act.activation(e, e, ACT.Exp).then_inc(sem["gs_ok"], 1)
                act.wait_ge(sem["lev_lo"], LEVELS * u + 5)
                act.activation(xq, cum, ACT.Exp).then_inc(sem["qe_e"], 1)
                act.wait_ge(sem["state_ok"], (NT - 1) * (u + 1))
                act.wait_ge(sem["step_ps"], STEPS * u + 6)
                act.activation(pair_hi[:, STATES], flat(state), ACT.Copy).then_inc(sem["state_hi_ok"], 1)
                act.wait_ge(sem["qe_ok"], u + 1)
                act.wait_ge(sem["step_ps"], STEPS * u + 7)
                act.activation(pair_hi[:, DECAYED], xq, ACT.Copy).then_inc(sem["qe_hi_ok"], 1)
                stage_group(u + 1, 6)
                if not last:
                    softplus_tail(u + 1)
                act.wait_ge(sem["score_ok"], STEPS * (u + 1))
                act.activation(pair_hi[:, SCORES], flat(score), ACT.Copy).then_inc(sem["s_hi_ok"], 1)
                stage_group(u + 1, 7)
                for h in range(NH):
                    cols = slice(h * HALF, (h + 1) * HALF)
                    act.wait_ge(sem["out_ps"], NH * u + h + 1)
                    act.activation(xo[:, cols], o_ps[:, cols], ACT.Square).then_inc(sem["sq_ok"], 1)
                if not last:
                    make_key(u + 1)
                    decay_keys(u + 1)
                    split_v(u + 1)
                for h in range(NH):
                    cols = slice(h * HALF, (h + 1) * HALF)
                    act.wait_ge(sem["ss_ok"], NH * u + h + 1)
                    act.activation(xo[:, cols], k_ps[:, cols], ACT.Ln, bias=core.eps[:, 0:1],
                                   scale=1.0 / P).then_inc(sem["ln_ok"], 1)
                    act.wait_ge(sem["ln_ok"], NH * u + h + 1)
                    act.activation(xo[:, cols], xo[:, cols], ACT.Exp, scale=-0.5).then_inc(sem["rstd_ok"], 1)

            unit(0)
            with act.Fori(1, UNITS - 1) as u:
                unit(u)
            unit(UNITS - 1, last=True)

        @block.vector
        def _(dve):
            def gates(u):
                dve.wait_ge(sem["lz_ok"], u + 1)
                at_least(dve, sem["qe_lo_ok"], u)
                dve.scalar_tensor_tensor(out=x[:, 1], in0=stage[:, F], scalar=0.0, in1=e, op0=ALU.min,
                                         op1=ALU.subtract).then_inc(sem["logf_ok"], 1)
                dve.wait_ge(sem["logf_ok"], u + 1)
                dve.scalar_tensor_tensor(out=e, in0=stage[:, F], scalar=0.0, in1=e, op0=ALU.max,
                                         op1=ALU.add).then_inc(sem["sp_ok"], 1)
                for c in range(NT):
                    cols = slice(P * c, P * (c + 1))
                    dve.tensor_tensor_scan(cum[:, cols], core.ones[:], x[:, 1, cols], 0.0, ALU.mult,
                                           ALU.add).then_inc(sem["cum_ok"], 1)

            def decay_keys(u):
                dve.wait_ge(sem["cum_ok"], NT * (u + 1))
                at_least(dve, sem["lev_lo"], LEVELS * u - 1)
                dve.tensor_tensor(chunks(x[:, 0]), chunks(cum)[:, :, P - 1:P].to_broadcast([P, NT, P]), chunks(cum),
                                  ALU.subtract).then_inc(sem["kd_d"], 1)
                dve.wait_ge(sem["kd_e"], u + 1)
                dve.wait_ge(sem["key_ok"], u + 1)
                dve.tensor_tensor(x[:, 0], x[:, 0], key, ALU.mult).then_inc(sem["kd_ok"], 1)

            def split_v(u):
                for h in range(NH):
                    cols = slice(h * HALF, (h + 1) * HALF)
                    dve.wait_ge(sem["v_hi_ok"], NH * u + h + 1)
                    dve.tensor_tensor(v_lo[:, 4 * h:4 * h + 4], chunks(t_ps[:, cols]),
                                      f32(v_hi[:, 4 * h:4 * h + 4]), ALU.subtract).then_inc(sem["v_lo_ok"], 1)

            def exponent(u, l):
                h = P >> (l + 1)
                blocks = lambda ap: ap.rearrange("p (b t) -> p b t", t=2 * h)
                if l == 2:
                    dve.wait_ge(sem["kd_turned"], u + 1)
                elif l >= 3:
                    dve.wait_ge(sem["lev_lo"], LEVELS * u + l - 2)
                dve.tensor_tensor(blocks(x[:, slot(l)]), blocks(cum),
                                  blocks(cum)[:, :, h - 1:h].to_broadcast([P, S // (2 * h), 2 * h]),
                                  ALU.subtract).then_inc(sem["lev_d"], 1)

            def keep(u, s):
                dve.wait_ge(sem["step_ps"], STEPS * u + s + 1)
                at_least(dve, sem["score_ok"], STEPS * u + s)
                dve.sem_inc(sem["small_in"], 1)
                m = LEVELS if s == 0 else s - 1
                dve.copy_predicated(score[:], levels[:, m:m + 1].to_broadcast([P, NT, P]),
                                    chunks((t_ps, k_ps)[s % 2][:])).then_inc(sem["score_ok"], 1)

            for kt in range(KT):
                rms.add(dve, kt)
            dve.wait_ge(sem["const_in"], 32)
            dve.wait_ge(rms.ready, 1)
            norm.on_dve(dve)
            dve.wait_ge(sem["zeroed"], 1)
            gates(0)
            decay_keys(0)
            split_v(0)
            dve.wait_ge(sem["small_in"], 32)

            def unit(u, last=False):
                at_least(dve, sem["o_ok"], NH * u)
                exponent(u, 0)
                dve.wait_ge(sem["q_ok"], u + 1)
                dve.wait_ge(sem["key_ok"], u + 1)
                dve.tensor_tensor(e, key, q, ALU.mult).then_inc(sem["kq_ok"], 1)
                for l in range(LEVELS):
                    if l + 1 < LEVELS:
                        exponent(u, l + 1)
                    dve.wait_ge(sem["lev_e"], LEVELS * u + l + 1)
                    d = halves(x[:, slot(l)], l)
                    dve.tensor_tensor(d[:, :, 0], d[:, :, 0], halves(key, l)[:, :, 0], ALU.mult)
                    dve.tensor_tensor(d[:, :, 1], d[:, :, 1], halves(q, l)[:, :, 1], ALU.mult).then_inc(sem["lev_x"], 1)
                    if l == 0:
                        dve.wait_ge(sem["kdT_hi_ok"], u + 1)
                        dve.tensor_tensor(pair_lo[:, TURNED], k_ps[:], f32(pair_hi[:, TURNED]),
                                          ALU.subtract).then_inc(sem["kdT_lo_ok"], 1)
                    else:
                        keep(u, l - 1)
                    if l == 2:
                        dve.wait_ge(sem["upd_ok"], u + 1)
                        dve.wait_ge(sem["el_ok"], u + 1)
                        for c in range(NT - 1):
                            at_least(dve, sem["state_ok"], (NT - 1) * u + c)
                            dve.scalar_tensor_tensor(out=state[:, c + 1], in0=state[:, c], scalar=elast[:, c:c + 1],
                                                     in1=o_ps[:, P * c:P * (c + 1)], op0=ALU.mult,
                                                     op1=ALU.add).then_inc(sem["state_ok"], 1)
                    if l == 5:
                        dve.wait_ge(sem["gl_ok"], u + 1)
                        dve.scalar_tensor_tensor(out=e, in0=stage[:, G], scalar=0.0, in1=e, op0=ALU.min,
                                                 op1=ALU.subtract).then_inc(sem["ga_ok"], 1)
                dve.wait_ge(sem["gs_ok"], u + 1)
                dve.tensor_tensor(gz, stage[:, G], e, ALU.mult).then_inc(sem["silu_ok"], 1)
                dve.wait_ge(sem["qe_e"], u + 1)
                dve.tensor_tensor(xq, xq, q, ALU.mult).then_inc(sem["qe_ok"], 1)
                keep(u, STEPS - 2)
                dve.wait_ge(sem["state_hi_ok"], u + 1)
                dve.tensor_tensor(pair_lo[:, STATES], flat(state), f32(pair_hi[:, STATES]),
                                  ALU.subtract).then_inc(sem["state_lo_ok"], 1)
                keep(u, STEPS - 1)
                dve.wait_ge(sem["qe_hi_ok"], u + 1)
                dve.tensor_tensor(pair_lo[:, DECAYED], xq, f32(pair_hi[:, DECAYED]),
                                  ALU.subtract).then_inc(sem["qe_lo_ok"], 1)
                dve.wait_ge(sem["s_hi_ok"], u + 1)
                dve.tensor_tensor(pair_lo[:, SCORES], flat(score), f32(pair_hi[:, SCORES]),
                                  ALU.subtract).then_inc(sem["s_lo_ok"], 1)
                if not last:
                    gates(u + 1)
                    decay_keys(u + 1)
                    split_v(u + 1)
                for h in range(NH):
                    cols = slice(h * HALF, (h + 1) * HALF)
                    dve.wait_ge(sem["rstd_ok"], NH * u + h + 1)
                    dve.tensor_tensor(xo[:, cols], xo[:, cols], gz[:, cols], ALU.mult).then_inc(sem["rg_ok"], 1)
                    dve.wait_ge(sem["rg_ok"], NH * u + h + 1)
                    dve.scalar_tensor_tensor(out=oT[:, u, cols], in0=o_ps[:, cols], scalar=onorm[:, 0:1],
                                             in1=xo[:, cols], op0=ALU.mult, op1=ALU.mult).then_inc(sem["o_ok"], 1)

            unit(0)
            with dve.Fori(1, UNITS - 1) as u:
                unit(u)
            unit(UNITS - 1, last=True)

        @block.tensor
        def _(pe):
            def turn(u):
                for h in range(NH):
                    proj.freed(pe, u, V, h)
                at_least(pe, sem["score_ok"], STEPS * u - 1)
                turn_v(pe, stage[:, V], t_ps, core.ident[:], sem["v_turned"])

            pe.wait_ge(sem["zeroed"], 1)
            rms.sum(pe)
            proj.run_as_ready(pe, 0, F, norm.features)
            proj.run(pe, 0, V)
            pe.wait_ge(sem["const_in"], 32)
            turn(0)
            proj.run(pe, 0, Q)
            proj.run(pe, 0, G)

            def unit(u, last=False):
                def fill(first, end):
                    for n in range(first, end):
                        g, kt = n // KT, n % KT
                        proj.part(pe, u + 1, g // NH, g % NH, kt)

                fill(0, 8)
                pe.wait_ge(sem["kd_ok"], u + 1)
                at_least(pe, sem["ln_ok"], NH * u)
                for c in range(NT):
                    mm = pe.transpose(k_ps[:, P * c:P * (c + 1)], x[:, 0, P * c:P * (c + 1)], core.ident[:])
                mm.then_inc(sem["kd_turned"], 1)
                fill(8, 16)
                pe.wait_ge(sem["kq_ok"], u + 1)
                pe.wait_ge(sem["v_lo_ok"], NH * (u + 1))
                for h in range(NH):
                    mm = pe.matmul(t_ps[:, h * HALF:(h + 1) * HALF], core.ones[:], e[:, h * HALF:(h + 1) * HALF],
                                   start=True, stop=True)
                mm.then_inc(sem["step_ps"], 1)
                fill(16, 20)
                pe.wait_ge(sem["kdT_lo_ok"], u + 1)
                at_least(pe, sem["o_ok"], NH * u)
                for c in range(NT - 1):
                    cols = slice(P * c, P * (c + 1))
                    mm = product(pe, o_ps[:, cols], pair_hi[:, TURNED, cols], pair_lo[:, TURNED, cols], v_hi[:, c],
                                 v_lo[:, c], True, True)
                mm.then_inc(sem["upd_ok"], 1)
                fill(20, 24)
                for l in range(LEVELS):
                    pe.wait_ge(sem["lev_lo"], LEVELS * u + l + 1)
                    at_least(pe, sem["score_ok"], STEPS * u + l)
                    for c in range(NT):
                        cols = slice(P * c, P * (c + 1))
                        mm = product(pe, (k_ps, t_ps)[l % 2][:, cols], pair_hi[:, l % 3, cols], pair_lo[:, l % 3, cols],
                                     pair_hi[:, l % 3, cols], pair_lo[:, l % 3, cols], True, True)
                    mm.then_inc(sem["step_ps"], 1)
                    fill(24 + 5 * l, 29 + 5 * l)
                fill(59, 64)
                if not last:
                    turn(u + 1)
                pe.wait_ge(sem["state_lo_ok"], u + 1)
                pe.wait_ge(sem["qe_lo_ok"], u + 1)
                pe.wait_ge(sem["s_lo_ok"], u + 1)
                for c in range(NT):
                    cols = slice(P * c, P * (c + 1))
                    mm = product(pe, o_ps[:, cols], v_hi[:, c], v_lo[:, c], pair_hi[:, SCORES, cols],
                                 pair_lo[:, SCORES, cols], True, c == 0)
                    if c:
                        mm = product(pe, o_ps[:, cols], pair_hi[:, STATES, cols], pair_lo[:, STATES, cols],
                                     pair_hi[:, DECAYED, cols], pair_lo[:, DECAYED, cols], False, True)
                    if c % 4 == 3:
                        mm.then_inc(sem["out_ps"], 1)
                for h in range(NH):
                    cols = slice(h * HALF, (h + 1) * HALF)
                    pe.wait_ge(sem["sq_ok"], NH * u + h + 1)
                    pe.matmul(k_ps[:, cols], core.ones[:], xo[:, cols], start=True, stop=True).then_inc(sem["ss_ok"], 1)

            unit(0)
            with pe.Fori(1, UNITS - 1) as u:
                unit(u)
            unit(UNITS - 1, last=True)



def differential_phase(core, dram, oT, gates):
    nc, w_in = core.nc, dram["w_in_t"]
    with core.phase() as ctx:
        W = WeightStream(core, ctx, "daw", 3, 3, 1)
        proj = Projection(core, ctx, "dap", W, core.ps[3], (core.hT_hi, core.hT_lo), banks=1)
        (small_in, row_ok, row_sum, row_out, flip_ok, bias_ok, lam_step, bias_in, qk_hi_ok, qk_lo_ok, v_turned, v_hi_ok,
         v_lo_ok, lg_ps_ok, lg_ok, nm_ok, p_ok, comb_step, w_ok, turned_ok, wT_hi_ok, wT_lo_ok, pv_ok, o_copied, sq_ok,
         ss_ok, ln_ok, rstd_ok, o_ok, dve_open) = core.sems(" ".join("da_" + n for n in (
             "small_in row_ok row_sum row_out flip_ok bias_ok lam_step bias_in qk_hi_ok qk_lo_ok v_turned v_hi_ok "
             "v_lo_ok lg_ps_ok lg_ok nm_ok p_ok comb_step w_ok turned_ok wT_hi_ok wT_lo_ok pv_ok o_copied sq_ok "
             "ss_ok ln_ok rstd_ok o_ok dve_open").split()))
        gates_out, = core.sems("da_gates_out")
        stage = core.sb("da_stage", [P, 3, S], F32, ctx)
        qk_hi = core.sb("da_qk_hi", [P, 2, S], F32R, ctx)
        qk_lo = core.sb("da_qk_lo", [P, 2, S], F32R, ctx)
        v_hi = core.sb("da_v_hi", [P, NT, P], F32R, ctx)
        v_lo = core.sb("da_v_lo", [P, NT, P], F32R, ctx)
        lg = core.sb("da_lg", [P, 2, 2, S], F32, ctx)
        wT_hi = core.sb("da_wT_hi", [P, S], F32R, ctx)
        wT_lo = core.sb("da_wT_lo", [P, S], F32R, ctx)
        bias = core.sb("da_bias", [P, S], F32, ctx)
        hankel = core.sb("da_hankel", [P, S], F32, ctx)
        o_sb = core.sb("da_o_sb", [P, S], F32, ctx)
        rstd = core.sb("da_rstd", [P, S], F32, ctx)
        mx = core.sb("da_mx", [P, 2, 2], F32, ctx)
        nm = core.sb("da_nm", [P, 2, 2], F32, ctx)
        sm = core.sb("da_sm", [P, 2, 2], F32, ctx)
        rs = core.sb("da_rs", [P, 2, 2], F32, ctx)
        rl = core.sb("da_rl", [P, 2], F32, ctx)
        lam4 = core.sb("da_lam4", [P, 4, DH], F32, ctx)
        lam2 = core.sb("da_lam2", [P, 2], F32, ctx)
        neg_lam = core.sb("da_neg_lam", [P, 1], F32, ctx)
        onorm = core.sb("da_onorm", [P, 1], F32, ctx)
        table = lg[0:BUCKETS, 1, 0, 0:DA_HEADS]
        row_mask = lg[0:DA_HEADS, 0].rearrange("p m s -> p (m s)")[:, 0:BIAS_COLS]
        hot = core.sb("da_hot", [BUCKETS, BIAS_COLS], F32, ctx)
        row_dram = nc.dram_tensor("da_bias_rows", [DA_HEADS, BIAS_COLS], F32).ap()
        flip = core.sb("da_flip", [P, P], F32, ctx)
        t_ps = core.ps[2]
        ss_ps = (core.ps[3][:, 0:HALF], core.ps[3][:, HALF:S])
        o_ps = core.ps[3][:, HALF:S]
        GROUPS = 3 * NH
        FILL_AT = (0, 1, 2, 3, 4, 5)
        QUERY_HALF = NT // NH

        def tile(i):
            return NT - 1 - i

        def keys(i):
            return P * (tile(i) + 1)

        def half(h):
            return slice((NH - 1 - h) * HALF, (NH - h) * HALF)

        block = ctx.enter_context(nc.Block())

        @block.sync
        def _(sp):
            def load(u, t):
                W.load(sp, u, t, w_in[GATE_TILE[2] + t if is_gates(u) else DA_TILES[t] + u])

            def load_bias(u):
                at_least(sp, flip_ok, u)
                src = row_dram[u, 0:S]
                src = bass.AP(src.tensor, src.offset, [[1, P], [1, S]])
                sp.dma_start(hankel[:], src).then_inc(bias_in, 16)

            load(0, 0)
            for dst, src in ((hot[:], dram["da_hot"]), (table, dram["rel_bias"]), (row_mask, dram["da_row_mask"]),
                             (lam4[:], dram["lam"].partition_broadcast(P)), (onorm[:], dram["da_onorm"]), (flip[:], dram["flip"])):
                sp.dma_start(dst, src).then_inc(small_in, 16)
            load(0, 1)
            load(0, 2)
            sp.wait_ge(row_sum, 3)
            sp.dma_start(row_dram, row_mask).then_inc(row_out, 16)
            load(1, 0)
            sp.wait_ge(row_out, 16)
            load_bias(0)

            def unit(u):
                load_bias(u + 1)
                load(u + 1, 1)
                load(u + 1, 2)
                load(u + 2, 0)

            unit(0)
            with sp.Fori(1, UNITS - 2) as u:
                unit(u)
            unit(UNITS - 2)
            load(UNITS, 1)
            load(UNITS, 2)
            store_gates(sp, proj, stage, gates, gates_out)

        @block.gpsimd
        def _(pool):
            def unit(u):
                for t in range(3):
                    proj.weights(pool, u, t)

            unit(0)
            with pool.Fori(1, UNITS + 1) as u:
                unit(u)

        @block.scalar
        def _(act):
            act.preload_act_table_set(EXP_LN)

            def stage_group(u, g):
                t = g // NH
                at_least(act, qk_lo_ok if t < 2 else v_turned, NH * u)
                stage_half(act, proj, stage[:, t], u, t, g % NH, QK_SCALE if t == 0 and not is_gates(u) else 1.0)

            def split_qk(u, t):
                act.wait_ge(proj.free[0], GROUPS * u + NH * (t + 1))
                at_least(act, lg_ps_ok, 2 * NT * u)
                act.activation(qk_hi[:, t], stage[:, t], ACT.Copy).then_inc(qk_hi_ok, 1)

            def copy_bias(u):
                act.wait_ge(flip_ok, u + 1)
                at_least(act, lg_ok, 2 * NT * u)
                act.activation(bias[:], core.ps[0][:], ACT.Copy).then_inc(bias_ok, 1)

            def split_v(u):
                for h in range(NH):
                    act.wait_ge(v_turned, NH * u + h + 1)
                    at_least(act, pv_ok, NT * u)
                    act.activation(v_hi[:, 4 * h:4 * h + 4, :],
                                   t_ps[:, h * HALF:(h + 1) * HALF].rearrange("p (a b) -> p a b", a=4),
                                   ACT.Copy).then_inc(v_hi_ok, 1)

            def square(u, h):
                cols = half(h)
                act.wait_ge(pv_ok, NT * u + QUERY_HALF * (h + 1))
                at_least(act, o_ok, NH * u)
                act.activation(rstd[:, cols], o_ps, ACT.Square).then_inc(sq_ok, 1)
                act.activation(o_sb[:, cols], o_ps, ACT.Copy).then_inc(o_copied, 1)

            def root(u, h):
                cols = half(h)
                act.wait_ge(ss_ok, NH * u + h + 1)
                act.activation(rstd[:, cols], ss_ps[h], ACT.Ln, bias=core.eps[:, 0:1],
                               scale=1.0 / P).then_inc(ln_ok, 1)
                act.wait_ge(ln_ok, NH * u + h + 1)
                act.activation(rstd[:, cols], rstd[:, cols], ACT.Exp, scale=-0.5).then_inc(rstd_ok, 1)

            for g in range(GROUPS):
                stage_group(0, g)
            for t in range(2):
                split_qk(0, t)
            split_v(0)
            copy_bias(0)
            act.wait_ge(lam_step, 2)
            act.activation(lam2[:], lam2[:], ACT.Exp).then_inc(lam_step, 1)

            def unit(u, last=False):
                for i in range(NT + 1):
                    if i < NT:
                        n = keys(i)
                        act.wait_ge(nm_ok, NT * u + i + 1)
                        for m in range(2):
                            x = lg[:, i % 2, m, 0:n]
                            act.activation(x, x, ACT.Exp, bias=nm[:, i % 2, m:m + 1],
                                           accum_out=sm[:, i % 2, m:m + 1]).then_inc(p_ok, 1)
                    if i == QUERY_HALF + 1:
                        square(u, 0)
                    if i >= 1:
                        n = keys(i - 1)
                        act.wait_ge(turned_ok, NT * u + i)
                        at_least(act, pv_ok, NT * u + i - 1)
                        act.activation(wT_hi[:, 0:n], t_ps[:, 0:n], ACT.Copy).then_inc(wT_hi_ok, 1)
                    if i - 1 in FILL_AT:
                        stage_group(u + 1, FILL_AT.index(i - 1))
                    if i == NT - 1 and not last:
                        for t in range(2):
                            split_qk(u + 1, t)
                root(u, 0)
                square(u, 1)
                if not last:
                    copy_bias(u + 1)
                    split_v(u + 1)
                root(u, 1)

            unit(0)
            with act.Fori(1, UNITS - 1) as u:
                unit(u)
            unit(UNITS - 1, last=True)

        @block.vector
        def _(dve):
            dve.wait_ge(small_in, 16 * 6)
            dve.tensor_tensor(lam4[:, 0:4:2], lam4[:, 0:4:2], lam4[:, 1:4:2], ALU.mult).then_inc(lam_step, 1)
            dve.wait_ge(lam_step, 1)
            dve.tensor_reduce(lam2[:], lam4[:, 0:4:2], AX.X, ALU.add).then_inc(lam_step, 1)
            dve.tensor_scalar(onorm[:], onorm[:], 1.0 - LAM_INIT, None, ALU.mult).then_inc(comb_step, 1)
            for b, (lo, hi) in enumerate(bias_chunks()):
                dve.wait_ge(row_ok, 3)
                dve.tensor_tensor(row_mask[:, lo:hi], bias_bank(core, b)[0:DA_HEADS, 0:hi - lo], row_mask[:, lo:hi],
                                  ALU.add).then_inc(row_sum, 1)

            def split_qk(u):
                for t in range(2):
                    dve.wait_ge(qk_hi_ok, 2 * u + t + 1)
                    dve.tensor_tensor(qk_lo[:, t], stage[:, t], f32(qk_hi[:, t]), ALU.subtract).then_inc(qk_lo_ok, 1)

            def split_v(u):
                for h in range(NH):
                    dve.wait_ge(v_hi_ok, NH * u + h + 1)
                    dve.tensor_tensor(v_lo[:, 4 * h:4 * h + 4, :],
                                      t_ps[:, h * HALF:(h + 1) * HALF].rearrange("p (a b) -> p a b", a=4),
                                      f32(v_hi[:, 4 * h:4 * h + 4, :]), ALU.subtract).then_inc(v_lo_ok, 1)

            split_qk(0)
            split_v(0)
            dve.wait_ge(lam_step, 3)
            dve.tensor_tensor(neg_lam[:], lam2[:, 1:2], lam2[:, 0:1], ALU.subtract).then_inc(lam_step, 1)
            dve.wait_ge(lam_step, 4)
            dve.tensor_scalar(neg_lam[:], neg_lam[:], -LAM_INIT, None, ALU.add).then_inc(lam_step, 1)

            def unit(u, last=False):
                dve.wait_ge(bias_ok, u + 1)
                for i in range(NT + 2):
                    if i < NT:
                        n, s = keys(i), i % 2
                        for m in range(2):
                            dve.wait_ge(lg_ps_ok, 2 * (NT * u + i) + m + 1)
                            at_least(dve, turned_ok, NT * u + i - 1)
                            dve.sem_inc(dve_open, 1)
                            dve.tensor_tensor_reduce(lg[:, s, m, 0:n], core.ps[m][:, 0:n], bias[:, S - n:S],
                                                     1.0, 3 * NEG, ALU.add, ALU.max,
                                                     mx[:, s, m:m + 1]).then_inc(lg_ok, 1)
                        dve.wait_ge(lg_ok, 2 * (NT * u + i + 1))
                        dve.tensor_scalar(nm[:, s], mx[:, s], -1.0, None, ALU.mult).then_inc(nm_ok, 1)
                    if i >= 2:
                        n = keys(i - 2)
                        dve.wait_ge(wT_hi_ok, NT * u + i - 1)
                        dve.tensor_tensor(wT_lo[:, 0:n], t_ps[:, 0:n], f32(wT_hi[:, 0:n]),
                                          ALU.subtract).then_inc(wT_lo_ok, 1)
                    if 1 <= i <= NT:
                        n, s, g = keys(i - 1), (i - 1) % 2, NT * u + i
                        dve.wait_ge(p_ok, 2 * g)
                        dve.reciprocal(rs[:, s], sm[:, s]).then_inc(comb_step, 1)
                        dve.wait_ge(comb_step, 3 * g - 1)
                        dve.tensor_tensor(rl[:, s:s + 1], rs[:, s, 1:2], neg_lam[:], ALU.mult).then_inc(comb_step, 1)
                        dve.tensor_scalar(lg[:, s, 0, 0:n], lg[:, s, 0, 0:n], rs[:, s, 0:1], None,
                                          ALU.mult).then_inc(comb_step, 1)
                        dve.wait_ge(comb_step, 3 * g + 1)
                        dve.scalar_tensor_tensor(out=lg[:, s, 0, 0:n], in0=lg[:, s, 1, 0:n], scalar=rl[:, s:s + 1],
                                                 in1=lg[:, s, 0, 0:n], op0=ALU.mult, op1=ALU.add).then_inc(w_ok, 1)
                    if i == NT and not last:
                        split_qk(u + 1)
                if not last:
                    split_v(u + 1)
                for h in range(NH):
                    cols = half(h)
                    dve.wait_ge(rstd_ok, NH * u + h + 1)
                    dve.wait_ge(o_copied, NH * u + h + 1)
                    dve.scalar_tensor_tensor(out=oT[:, u, cols], in0=o_sb[:, cols], scalar=onorm[:, 0:1],
                                             in1=rstd[:, cols], op0=ALU.mult, op1=ALU.mult).then_inc(o_ok, 1)

            unit(0)
            with dve.Fori(1, UNITS - 1) as u:
                unit(u)
            unit(UNITS - 1, last=True)

        @block.tensor
        def _(pe):
            def logits(u, i):
                for m in range(2):
                    at_least(pe, lg_ok, 2 * (NT * u + i - 1) + m + 1)
                    rows, n = slice(DH * m, DH * (m + 1)), keys(i)
                    queries = slice(P * tile(i), P * (tile(i) + 1))
                    for lo in range(0, n, HALF):
                        hi = min(n, lo + HALF)
                        mm = product(pe, core.ps[m][:, lo:hi],
                                     qk_hi[rows, 0, queries], qk_lo[rows, 0, queries],
                                     qk_hi[rows, 1, lo:hi], qk_lo[rows, 1, lo:hi], True, True)
                    mm.then_inc(lg_ps_ok, 1)

            def turn_bias(u):
                pe.wait_ge(bias_in, 16 * (u + 1))
                at_least(pe, lg_ok, 2 * NT * u)
                for h in range(NH):
                    cols = slice(h * HALF, (h + 1) * HALF)
                    mm = pe.matmul(core.ps[0][:, cols], flip[:], hankel[:, cols], start=True, stop=True)
                mm.then_inc(flip_ok, 1)

            def sum_squares(u, h):
                pe.wait_ge(sq_ok, NH * u + h + 1)
                if h:
                    pe.wait_ge(o_copied, NH * u + h + 1)
                pe.matmul(ss_ps[h], core.ones[:], rstd[:, half(h)],
                          start=True, stop=True).then_inc(ss_ok, 1)

            proj.run(pe, 0, 0)
            pe.wait_ge(small_in, 16 * 6)
            for b, (lo, hi) in enumerate(bias_chunks()):
                pe.matmul(bias_bank(core, b)[0:DA_HEADS, 0:hi - lo], table, hot[:, lo:hi],
                          start=True, stop=True).then_inc(row_ok, 1)
            proj.run(pe, 0, 1)
            proj.run(pe, 0, 2)
            proj.freed(pe, 0, 2, 1)
            turn_v(pe, stage[:, 2], t_ps, core.ident[:], v_turned)
            pe.wait_ge(row_sum, 3)
            turn_bias(0)

            def unit(u, last=False):
                pe.wait_ge(bias_ok, u + 1)
                pe.wait_ge(qk_lo_ok, 2 * (u + 1))
                logits(u, 0)
                for i in range(NT + 1):
                    if i + 1 < NT:
                        logits(u, i + 1)
                    if i in FILL_AT:
                        g = FILL_AT.index(i)
                        if i == 0:
                            at_least(pe, ln_ok, NH * u - 1)
                        for kt in range(KT):
                            proj.part(pe, u + 1, g // NH, g % NH, kt)
                    if i >= 1:
                        if i == 1:
                            pe.wait_ge(v_lo_ok, NH * (u + 1))
                            at_least(pe, ln_ok, NH * u)
                        if i == QUERY_HALF + 1:
                            pe.wait_ge(o_copied, NH * u + 1)
                        pe.wait_ge(wT_lo_ok, NT * u + i)
                        q = tile(i - 1) % QUERY_HALF
                        for j in range(tile(i - 1) + 1):
                            cols = slice(P * j, P * (j + 1))
                            mm = product(pe, o_ps[:, P * q:P * (q + 1)], v_hi[:, j], v_lo[:, j],
                                         wT_hi[:, cols], wT_lo[:, cols], j == 0, j == tile(i - 1))
                        mm.then_inc(pv_ok, 1)
                    if i < NT:
                        pe.wait_ge(w_ok, NT * u + i + 1)
                        if i == 0:
                            pe.wait_ge(v_lo_ok, NH * (u + 1))
                        for j in range(tile(i) + 1):
                            mm = pe.transpose(t_ps[:, P * j:P * (j + 1)], lg[:, i % 2, 0, P * j:P * (j + 1)],
                                              core.ident[:])
                        mm.then_inc(turned_ok, 1)
                    if i == NT - 1 + (FILL_AT[-1] == NT - 1):
                        proj.freed(pe, u + 1, 2, 1)
                        sum_squares(u, 0)
                if not last:
                    turn_bias(u + 1)
                    turn_v(pe, stage[:, 2], t_ps, core.ident[:], v_turned)
                sum_squares(u, 1)

            unit(0)
            with pe.Fori(1, UNITS - 1) as u:
                unit(u)
            unit(UNITS - 1, last=True)


def bias_chunks():
    return [(lo, min(BIAS_COLS, lo + HALF)) for lo in range(0, BIAS_COLS, HALF)]


def bias_bank(core, b):
    return core.ps[b // 2][:, (b % 2) * HALF:(b % 2 + 1) * HALF]


def program(nc, dram, out):
    with ExitStack() as ctx:
        core = Core(nc, ctx)
        merged = nc.dram_tensor("merged", [2, KT, P, S], F32).ap()
        gates = [nc.dram_tensor(f"gates{b}", [n, P, S], F32).ap() for b, n in enumerate(EARLY_GATES)]
        w_in, w_branch = dram["w_in_t"], dram["w_branch_t"]
        oT = core.sb("oT", [P, BT, S], F32)
        hgrn2_phase(core, dram, oT, gates[0])
        merge_phase(core, 0, w_in, w_branch, oT, gates[0], merged)
        stick_breaking_phase(core, dram, oT, gates[1])
        merge_phase(core, 1, w_in, w_branch, oT, gates[1], merged)
        differential_phase(core, dram, oT, gates[2])
        core.R = core.sb("R", [P, KT, S], F32)
        merge_phase(core, 2, w_in, w_branch, oT, gates[2], merged)
        core.rstd = core.sb("rstd", [P, S], F32)
        out_phase(core, dram["w_out_t"], dram["xT"])
        mlp_phase(core, dram["w_up_t"], dram["w_down_t"], dram["conv"], oT, out)


def host_constants():
    i = np.arange(P)
    key, query = i[:, None], i[None, :]
    eye = np.eye(P, dtype=np.float32)
    later = (key >= query).astype(np.float32)
    sb = np.stack([eye, later, 1 - later, np.where(key >= query, NEG, 0)], axis=1).astype(np.float32)
    dist = np.arange(S - 1, -P, -1)
    n = np.maximum(dist, 0)
    exact = BUCKETS // 2
    scaled = np.log(np.maximum(n, 1).astype(np.float32) / exact) / math.log(MAX_DIST / exact)
    large = np.minimum(exact + (scaled * (BUCKETS - exact)).astype(np.int32), BUCKETS - 1)
    bucket = np.where(n < exact, n, large)
    hot = (np.arange(BUCKETS)[:, None] == bucket[None, :]).astype(np.float32)
    row_mask = np.broadcast_to(np.where(dist < 0, NEG, 0).astype(np.float32), (DA_HEADS, BIAS_COLS))
    level = np.zeros((P, LEVELS + 1, P), np.int32)
    for l in range(LEVELS):
        h = P >> (l + 1)
        level[:, l] = (key // (2 * h) == query // (2 * h)) & (key % (2 * h) < h) & (query % (2 * h) >= h)
    level[:, LEVELS] = key == query
    return {"ident": eye, "flip": np.ascontiguousarray(eye[::-1]), "sb_masks": np.ascontiguousarray(sb), "da_hot": hot,
            "da_row_mask": np.ascontiguousarray(row_mask), "hg_levels": level}


def col_tiles(w):
    r, c = w.shape
    return np.ascontiguousarray(w.reshape(r // P, P, c // P, P).transpose(2, 1, 0, 3))


def kernel(**inputs):
    import concourse.bacc as bacc
    from concourse.bass_utils import run_bass_kernel_spmd as run
    a = {k: np.asarray(v) for k, v in inputs.items()}
    nc = bacc.Bacc("TRN2", target_bir_lowering=False, num_devices=1)
    feature_major = lambda x: np.ascontiguousarray(x.T.reshape(KT, P, S).transpose(1, 0, 2))
    arrays = {
        "xT": feature_major(a["x"][0]),
        "w_in_t": col_tiles(a["w_in"][0]),
        "norm_w": np.ascontiguousarray(np.stack([a["attn_norm_w"][0], a["ffn_norm_w"][0], a["final_norm_w"]])
                                       .reshape(3, KT, P).transpose(2, 0, 1)),
        "w_branch_t": np.stack([col_tiles(a[n][0]) for n in ("w_hgrn_out", "w_sb_out", "w_diff_out")]),
        "w_out_t": col_tiles(a["w_out"][0]),
        "w_up_t": col_tiles(a["w_up"][0]),
        "w_down_t": np.ascontiguousarray(a["w_down"][0].reshape(FT, P, KT, P)),
        "conv": np.ascontiguousarray(np.concatenate([a["conv_w"][0], a["conv_b"]])
                                     .reshape(4, 2 * FT, P).transpose(2, 1, 0)),
        "rel_bias": a["rel_bias"],
        "lam": a["diff_lambda"][0],
        "da_onorm": np.ascontiguousarray(a["diff_onorm_w"].T),
        "hg_onorm": np.ascontiguousarray(a["hgrn_onorm_w"].T),
        **host_constants(),
    }
    dram = {n: nc.dram_tensor("in_" + n, v.shape, mybir.dt.from_np(v.dtype), kind="ExternalInput").ap()
            for n, v in arrays.items()}
    out = nc.dram_tensor("out0", (P, KT, S), F32, kind="ExternalOutput").ap()
    program(nc, dram, out)
    rows = lambda y: np.ascontiguousarray(y.transpose(1, 0, 2).reshape(D, S).T)[None]
    r = run(nc, [{"in_" + n: v for n, v in arrays.items()}], core_ids=[0])
    return rows(r.results[0]["out0"])
```
